# Optimizing a Trainium2 kernel written in Bass

```python
import math
import jax, jax.numpy as jnp
from jax import lax
import numpy as np

D_MODEL = 1024
BATCH = 1
SEQ = 512
DEPTH = 2

QBLK = 128
NORM_EPS = 1e-6
ROPE_BASE = 10000.0
MAX_POS_OFFSET = 4096

A_HEADS = 8
A_HEAD_DIM = 64
IDX_HEADS = 4
IDX_DIM = 64
DSA_TOPK = 256
A_WIDTH = A_HEADS * A_HEAD_DIM
B_HEADS = 4
B_QK_DIM = 64
B_V_DIM = 128
RET_CHUNK = 128
B_WIDTH = B_HEADS * B_V_DIM
C_HEADS = 4
C_QK_DIM = 64
C_V_DIM = 128
C_WIDTH = C_HEADS * C_V_DIM
D_HEADS = 8
D_NOPE_DIM = 64
D_ROPE_DIM = 32
D_V_DIM = 64
D_Q_LORA = 256
D_KV_LORA = 128
D_WIDTH = D_HEADS * D_V_DIM

EVEN_MIX_WIDTH = A_WIDTH + B_WIDTH
ODD_MIX_WIDTH = C_WIDTH + D_WIDTH
EVEN_WIDTHS = (A_WIDTH, A_WIDTH, A_WIDTH, A_WIDTH,
               IDX_HEADS * IDX_DIM, IDX_DIM, IDX_HEADS,
               B_HEADS * B_QK_DIM, B_HEADS * B_QK_DIM,
               B_WIDTH, B_WIDTH)
ODD_WIDTHS = (C_HEADS * 2 * C_QK_DIM, C_HEADS * 2 * C_QK_DIM,
              C_WIDTH, C_WIDTH,
              D_Q_LORA, D_KV_LORA, D_ROPE_DIM, D_WIDTH)
EVEN_IN = sum(EVEN_WIDTHS)
ODD_IN = sum(ODD_WIDTHS)


def split_columns(h, widths):
    out, start = [], 0
    for w in widths:
        out.append(h[..., start:start + w])
        start += w
    return out

def rms_norm(x, gain=None):
    xf = x.astype(jnp.float32)
    y = xf * lax.rsqrt(jnp.mean(xf * xf, axis=-1, keepdims=True) + NORM_EPS)
    if gain is not None:
        y = y * gain.astype(jnp.float32)
    return y.astype(x.dtype)

def head_group_norm(x):
    xf = x.astype(jnp.float32)
    mu = jnp.mean(xf, axis=-1, keepdims=True)
    var = jnp.mean(jnp.square(xf - mu), axis=-1, keepdims=True)
    return ((xf - mu) * lax.rsqrt(var + NORM_EPS)).astype(x.dtype)

def rotary(x, positions):
    half = x.shape[-1] // 2
    inv_freq = ROPE_BASE ** (-jnp.arange(half, dtype=jnp.float32) / half)
    ang = positions.astype(jnp.float32)[:, :, None, None] * inv_freq
    cos, sin = jnp.cos(ang), jnp.sin(ang)
    xf = x.astype(jnp.float32)
    x1, x2 = xf[..., :half], xf[..., half:]
    return jnp.concatenate([x1 * cos - x2 * sin, x1 * sin + x2 * cos], axis=-1).astype(x.dtype)

def to_blocks(a, nb):
    b = a.shape[0]
    return a.reshape((b, nb, QBLK) + a.shape[2:]).swapaxes(0, 1)

def from_blocks(a):
    nb, b, q = a.shape[:3]
    return a.swapaxes(0, 1).reshape((b, nb * q) + a.shape[3:])

def causal_attention(q, k, v, scale):
    t = q.shape[1]
    nb = t // QBLK
    kpos = jnp.arange(t)

    def block(args):
        qb, i = args
        qpos = i * QBLK + jnp.arange(QBLK)
        s = jnp.einsum('bqhd,bkhd->bhqk', qb, k).astype(jnp.float32) * scale
        s = jnp.where((kpos[None, :] <= qpos[:, None])[None, None], s, -jnp.inf)
        p = jax.nn.softmax(s, axis=-1).astype(v.dtype)
        return jnp.einsum('bhqk,bkhd->bqhd', p, v)

    out = lax.map(block, (to_blocks(q, nb), jnp.arange(nb)))
    return from_blocks(out)

def dsa_attention(q, k, v, q_idx, k_idx, w_idx):
    b, t, h, d = q.shape
    topk = min(DSA_TOPK, t // 4)
    nb = t // QBLK
    kpos = jnp.arange(t)
    w_idx = w_idx * (IDX_HEADS ** -0.5 * IDX_DIM ** -0.5)
    gather = jax.vmap(lambda a, ix: a[ix])

    def block(args):
        qb, qib, wb, i = args
        qpos = i * QBLK + jnp.arange(QBLK)
        causal = kpos[None, :] <= qpos[:, None]
        rel = jax.nn.relu(jnp.einsum('bqhd,bsd->bqhs', qib, k_idx))
        score = jnp.einsum('bqh,bqhs->bqs', wb, rel).astype(jnp.float32)
        score = jnp.where(causal[None], score, -jnp.inf)
        _, sel = lax.top_k(score, topk)
        valid = sel <= qpos[None, :, None]
        ks = gather(k, sel).reshape(b, QBLK, topk, h, d)
        vs = gather(v, sel).reshape(b, QBLK, topk, h, d)
        s = jnp.einsum('bqhd,bqkhd->bqhk', qb, ks).astype(jnp.float32) * (d ** -0.5)
        s = jnp.where(valid[:, :, None, :], s, -jnp.inf)
        p = jax.nn.softmax(s, axis=-1).astype(vs.dtype)
        return jnp.einsum('bqhk,bqkhd->bqhd', p, vs)

    out = lax.map(block, (to_blocks(q, nb), to_blocks(q_idx, nb), to_blocks(w_idx, nb), jnp.arange(nb)))
    return from_blocks(out).reshape(b, t, h * d)

def retention(q, k, v):
    b, t, h, dk = q.shape
    dv = v.shape[-1]
    c = RET_CHUNK
    n = t // c
    gammas = 1.0 - 2.0 ** (-5.0 - jnp.arange(h, dtype=jnp.float32))
    log_g = jnp.log(gammas)
    q = q.reshape(b, n, c, h, dk)
    k = k.reshape(b, n, c, h, dk)
    v = v.reshape(b, n, c, h, dv)
    idx = jnp.arange(c)
    diff = idx[:, None] - idx[None, :]
    decay = jnp.where(diff[None] >= 0, jnp.exp(diff[None].astype(jnp.float32) * log_g[:, None, None]), 0.0)
    s = jnp.einsum('bnihd,bnjhd->bnhij', q, k) * decay
    intra = jnp.einsum('bnhij,bnjhe->bnihe', s, v)
    zeta = jnp.exp((c - 1 - idx).astype(jnp.float32)[:, None] * log_g[None, :])
    xi = jnp.exp((idx + 1).astype(jnp.float32)[:, None] * log_g[None, :])
    u = jnp.einsum('bnjhd,jh,bnjhe->nbhde', k, zeta, v)
    g_chunk = jnp.exp(c * log_g)[None, :, None, None]

    def step(state, inc):
        return g_chunk * state + inc, state

    _, s_prev = lax.scan(step, jnp.zeros((b, h, dk, dv), u.dtype), u)
    cross = jnp.einsum('bnihd,ih,nbhde->bnihe', q, xi, s_prev)
    return (intra + cross).reshape(b, t, h, dv).astype(v.dtype)

def even_mixer(h, positions, w_in, w_out):
    b, t, _ = h.shape
    (aq, ak, av, ag, iq, ik, iw, bq, bk, bv, bg) = split_columns(h @ w_in, EVEN_WIDTHS)
    a = dsa_attention(aq.reshape(b, t, A_HEADS, A_HEAD_DIM), ak, av,
                      iq.reshape(b, t, IDX_HEADS, IDX_DIM), ik, iw)
    a = a * jax.nn.silu(ag)
    q = rotary(bq.reshape(b, t, B_HEADS, B_QK_DIM), positions)
    k = rotary(bk.reshape(b, t, B_HEADS, B_QK_DIM), positions) * (B_QK_DIM ** -0.5)
    r = head_group_norm(retention(q, k, bv.reshape(b, t, B_HEADS, B_V_DIM)))
    r = r.reshape(b, t, B_WIDTH) * jax.nn.silu(bg)
    return jnp.concatenate([a, r], axis=-1) @ w_out

def odd_mixer(h, positions, w_in, w_out, lam_params, subln, q_norm, kv_norm, w_uq, w_ukv, layer):
    b, t, _ = h.shape
    (cq, ck, cv, cg, dcq, dckv, dkr, dg) = split_columns(h @ w_in, ODD_WIDTHS)
    q = cq.reshape(b, t, C_HEADS, 2 * C_QK_DIM)
    k = ck.reshape(b, t, C_HEADS, 2 * C_QK_DIM)
    v = cv.reshape(b, t, C_HEADS, C_V_DIM)
    qs = jnp.concatenate([q[..., :C_QK_DIM], q[..., C_QK_DIM:]], axis=2)
    ks = jnp.concatenate([k[..., :C_QK_DIM], k[..., C_QK_DIM:]], axis=2)
    o = causal_attention(qs, ks, jnp.concatenate([v, v], axis=2), C_QK_DIM ** -0.5)
    lam_init = 0.8 - 0.6 * math.exp(-0.3 * layer)
    lam = (jnp.exp(jnp.sum(lam_params[0] * lam_params[1]))
           - jnp.exp(jnp.sum(lam_params[2] * lam_params[3])) + lam_init)
    c = rms_norm(o[:, :, :C_HEADS] - lam * o[:, :, C_HEADS:], subln) * (1.0 - lam_init)
    c = c.reshape(b, t, C_WIDTH) * jax.nn.silu(cg)
    qd = (rms_norm(dcq, q_norm) @ w_uq).reshape(b, t, D_HEADS, D_NOPE_DIM + D_ROPE_DIM)
    kv = (rms_norm(dckv, kv_norm) @ w_ukv).reshape(b, t, D_HEADS, D_NOPE_DIM + D_V_DIM)
    q_full = jnp.concatenate([qd[..., :D_NOPE_DIM], rotary(qd[..., D_NOPE_DIM:], positions)], axis=-1)
    k_rope = jnp.broadcast_to(rotary(dkr[:, :, None, :], positions), (b, t, D_HEADS, D_ROPE_DIM))
    k_full = jnp.concatenate([kv[..., :D_NOPE_DIM], k_rope], axis=-1)
    m = causal_attention(q_full, k_full, kv[..., D_NOPE_DIM:], (D_NOPE_DIM + D_ROPE_DIM) ** -0.5)
    m = m.reshape(b, t, D_WIDTH) * jax.nn.silu(dg)
    return jnp.concatenate([c, m], axis=-1) @ w_out

def first_inputs(seed: int = 0) -> dict:
    key = jax.random.key(seed)
    ks = jax.random.split(key, 16)
    n_even = (DEPTH + 1) // 2
    n_odd = DEPTH // 2
    nrm = jax.random.normal
    f32 = jnp.float32
    x = nrm(ks[0], (BATCH, SEQ, D_MODEL), f32)
    offset = jax.random.randint(ks[1], (BATCH, 1), 0, MAX_POS_OFFSET)
    positions = (offset + jnp.arange(SEQ)[None, :]).astype(jnp.int32)
    return {
        'x': x,
        'positions': positions,
        'pre_norm': 1.0 + 0.02 * nrm(ks[2], (DEPTH, D_MODEL), f32),
        'post_norm': 1.0 + 0.02 * nrm(ks[3], (DEPTH, D_MODEL), f32),
        'w_in_even': nrm(ks[4], (n_even, D_MODEL, EVEN_IN), f32) * D_MODEL ** -0.5,
        'w_out_even': nrm(ks[5], (n_even, EVEN_MIX_WIDTH, D_MODEL), f32) * EVEN_MIX_WIDTH ** -0.5,
        'w_in_odd': nrm(ks[6], (n_odd, D_MODEL, ODD_IN), f32) * D_MODEL ** -0.5,
        'diff_lambda': 0.1 * nrm(ks[7], (n_odd, 4, C_QK_DIM), f32),
        'diff_subln': 1.0 + 0.02 * nrm(ks[8], (n_odd, C_V_DIM), f32),
        'mla_q_norm': 1.0 + 0.02 * nrm(ks[9], (n_odd, D_Q_LORA), f32),
        'mla_kv_norm': 1.0 + 0.02 * nrm(ks[10], (n_odd, D_KV_LORA), f32),
        'mla_w_uq': nrm(ks[11], (n_odd, D_Q_LORA, D_HEADS * (D_NOPE_DIM + D_ROPE_DIM)), f32) * D_Q_LORA ** -0.5,
        'mla_w_ukv': nrm(ks[12], (n_odd, D_KV_LORA, D_HEADS * (D_NOPE_DIM + D_V_DIM)), f32) * D_KV_LORA ** -0.5,
        'w_out_odd': nrm(ks[13], (n_odd, ODD_MIX_WIDTH, D_MODEL), f32) * ODD_MIX_WIDTH ** -0.5,
    }

def first_block(x, positions, pre_norm, post_norm, w_in_even, w_out_even, w_in_odd,
              diff_lambda, diff_subln, mla_q_norm, mla_kv_norm, mla_w_uq, mla_w_ukv, w_out_odd):
    for layer in range(DEPTH):
        h = rms_norm(x, pre_norm[layer])
        j = layer // 2
        if layer % 2 == 0:
            m = even_mixer(h, positions, w_in_even[j], w_out_even[j])
        else:
            m = odd_mixer(h, positions, w_in_odd[j], w_out_odd[j], diff_lambda[j], diff_subln[j],
                          mla_q_norm[j], mla_kv_norm[j], mla_w_uq[j], mla_w_ukv[j], layer)
        x = x + rms_norm(m, post_norm[layer])
    return x


DEPTH_2 = 1

CHUNK = 64
EPS = 1e-6
HG_HEADS = 8
HG_DK = 128
HG_DV = D_MODEL // HG_HEADS
HG_WIDTH_K = HG_HEADS * HG_DK
HG_WIDTH_V = HG_HEADS * HG_DV
GDN_QK_HEADS = 8
GDN_V_HEADS = 16
GDN_DK = 128
GDN_DV = 128
GDN_WIDTH_K = GDN_QK_HEADS * GDN_DK
GDN_WIDTH_V = GDN_V_HEADS * GDN_DV
CONV_K = 4
D_FF = 2816
IN_SIZES = (HG_WIDTH_K, HG_WIDTH_K, HG_WIDTH_V, HG_WIDTH_V,
            GDN_WIDTH_K, GDN_WIDTH_K, GDN_WIDTH_V, GDN_V_HEADS, GDN_V_HEADS, GDN_WIDTH_V,
            D_MODEL, D_MODEL)
IN_WIDTH = sum(IN_SIZES)


def rmsnorm(x, g):
    xf = x.astype(jnp.float32)
    y = xf * lax.rsqrt(jnp.mean(xf * xf, axis=-1, keepdims=True) + EPS)
    return (y * g).astype(x.dtype)

def l2norm(x):
    return x * lax.rsqrt(jnp.sum(x * x, axis=-1, keepdims=True) + EPS)

def swiglu(x, w_in, w_out):
    a, b = jnp.split(x @ w_in, 2, axis=-1)
    return (jax.nn.silu(a) * b) @ w_out

def to_chunks(t, n_heads):
    B, S = t.shape[:2]
    t = t.reshape(B, S // CHUNK, CHUNK, n_heads, -1)
    return jnp.transpose(t, (0, 3, 1, 2, 4))

def from_chunks(t):
    B, H, NC, C, d = t.shape
    return jnp.transpose(t, (0, 2, 3, 1, 4)).reshape(B, NC * C, H, d)

def causal_short_conv(x, w):
    K = w.shape[0]
    S = x.shape[1]
    xp = jnp.pad(x, ((0, 0), (K - 1, 0), (0, 0)))
    return sum(xp[:, j:j + S] * w[j] for j in range(K))

def hgrn2_chunked(q, k, v, log_f):
    B, H, NC, C, DK = q.shape
    DV = v.shape[-1]
    b_cum = jnp.cumsum(log_f, axis=3)
    causal = jnp.tril(jnp.ones((C, C), dtype=bool))[:, :, None]

    def step(S, inp):
        q_c, k_c, v_c, b_c = inp
        inter = jnp.einsum('bhtk,bhkv->bhtv', q_c * jnp.exp(b_c), S)
        diff = b_c[:, :, :, None, :] - b_c[:, :, None, :, :]
        decay = jnp.exp(jnp.where(causal, diff, -jnp.inf))
        scores = jnp.einsum('bhtk,bhsk,bhtsk->bhts', q_c, k_c, decay)
        intra = jnp.einsum('bhts,bhsv->bhtv', scores, v_c)
        b_end = b_c[:, :, -1, :]
        k_to_end = k_c * jnp.exp(b_end[:, :, None, :] - b_c)
        S = jnp.exp(b_end)[..., None] * S + jnp.einsum('bhsk,bhsv->bhkv', k_to_end, v_c)
        return S, inter + intra

    S0 = jnp.zeros((B, H, DK, DV), jnp.float32)
    xs = (jnp.moveaxis(q, 2, 0), jnp.moveaxis(k, 2, 0), jnp.moveaxis(v, 2, 0), jnp.moveaxis(b_cum, 2, 0))
    _, o = lax.scan(step, S0, xs)
    return jnp.moveaxis(o, 0, 2)

def gated_delta_chunked(q, k, v, beta, g):
    B, H, NC, C, DK = q.shape
    DV = v.shape[-1]
    gam = jnp.cumsum(g, axis=-1)
    incl = jnp.tril(jnp.ones((C, C), dtype=bool))
    strict = jnp.tril(jnp.ones((C, C), dtype=bool), -1)
    diff = gam[..., :, None] - gam[..., None, :]
    Lmat = jnp.exp(jnp.where(incl, diff, -jnp.inf))
    kb = k * beta[..., None]
    A = jnp.where(strict, jnp.einsum('bhntk,bhnsk->bhnts', kb, k) * Lmat, 0.0)
    eye = jnp.eye(C, dtype=A.dtype)
    T = lax.linalg.triangular_solve(eye + A, jnp.broadcast_to(eye, A.shape),
                                    left_side=True, lower=True, unit_diagonal=True)
    u = jnp.matmul(T, v * beta[..., None])
    w = jnp.matmul(T, kb * jnp.exp(gam)[..., None])
    qk = jnp.einsum('bhntk,bhnsk->bhnts', q, k) * Lmat

    def step(S, inp):
        q_c, k_c, u_c, w_c, qk_c, gam_c = inp
        v_new = u_c - jnp.einsum('bhtk,bhkv->bhtv', w_c, S)
        o = (jnp.einsum('bhtk,bhkv->bhtv', q_c * jnp.exp(gam_c)[..., None], S)
             + jnp.einsum('bhts,bhsv->bhtv', qk_c, v_new))
        g_end = gam_c[..., -1]
        k_to_end = k_c * jnp.exp(g_end[..., None] - gam_c)[..., None]
        S = S * jnp.exp(g_end)[..., None, None] + jnp.einsum('bhsk,bhsv->bhkv', k_to_end, v_new)
        return S, o

    S0 = jnp.zeros((B, H, DK, DV), jnp.float32)
    xs = tuple(jnp.moveaxis(t, 2, 0) for t in (q, k, u, w, qk, gam))
    _, o = lax.scan(step, S0, xs)
    return jnp.moveaxis(o, 0, 2)

def hybrid_mixer(u, w_in, lb, hgrn_out_norm, conv_w, a_log, dt_bias, gdn_out_norm,
                 w_branch_hgrn, w_branch_gdn, w_out):
    B, S, _ = u.shape
    f32 = jnp.float32
    proj = (u @ w_in).astype(f32)
    offsets = np.cumsum(IN_SIZES)[:-1].tolist()
    (hq, hf, hi, hg, gq, gk, gv, ga, gb, gz, gate_h, gate_g) = jnp.split(proj, offsets, axis=-1)

    lb = lb.astype(f32)
    log_f = jnp.logaddexp(jnp.log(lb), jnp.log1p(-lb) + jax.nn.log_sigmoid(hf))
    k_h = -jnp.expm1(log_f)
    q_h = jax.nn.silu(hq) * HG_DK ** -0.5
    o_h = hgrn2_chunked(to_chunks(q_h, HG_HEADS), to_chunks(k_h, HG_HEADS),
                        to_chunks(hi, HG_HEADS), to_chunks(log_f, HG_HEADS))
    o_h = rmsnorm(from_chunks(o_h), hgrn_out_norm) * jax.nn.silu(hg).reshape(B, S, HG_HEADS, HG_DV)
    y_h = o_h.reshape(B, S, HG_WIDTH_V) @ w_branch_hgrn

    qkv = jax.nn.silu(causal_short_conv(jnp.concatenate([gq, gk, gv], axis=-1), conv_w))
    cq, ck, cv = jnp.split(qkv, [GDN_WIDTH_K, 2 * GDN_WIDTH_K], axis=-1)
    rep = GDN_V_HEADS // GDN_QK_HEADS
    q_g = l2norm(cq.reshape(B, S, GDN_QK_HEADS, GDN_DK)) * GDN_DK ** -0.5
    k_g = l2norm(ck.reshape(B, S, GDN_QK_HEADS, GDN_DK))
    q_g = jnp.repeat(q_g, rep, axis=2).reshape(B, S, GDN_V_HEADS * GDN_DK)
    k_g = jnp.repeat(k_g, rep, axis=2).reshape(B, S, GDN_V_HEADS * GDN_DK)
    beta = jax.nn.sigmoid(gb)
    g = -jnp.exp(a_log.astype(f32)) * jax.nn.softplus(ga + dt_bias)
    o_g = gated_delta_chunked(to_chunks(q_g, GDN_V_HEADS), to_chunks(k_g, GDN_V_HEADS),
                              to_chunks(cv, GDN_V_HEADS),
                              to_chunks(beta[..., None], GDN_V_HEADS)[..., 0],
                              to_chunks(g[..., None], GDN_V_HEADS)[..., 0])
    o_g = rmsnorm(from_chunks(o_g), gdn_out_norm) * jax.nn.silu(gz).reshape(B, S, GDN_V_HEADS, GDN_DV)
    y_g = o_g.reshape(B, S, GDN_WIDTH_V) @ w_branch_gdn

    y = jax.nn.sigmoid(gate_h) * y_h + jax.nn.sigmoid(gate_g) * y_g
    return (y @ w_out).astype(u.dtype)

def second_inputs(seed: int = 0) -> dict:
    key = jax.random.key(seed)
    ks = jax.random.split(key, 20)
    f32 = jnp.float32
    L = DEPTH_2

    def dense(k, shape):
        return jax.random.normal(k, shape, f32) * shape[-2] ** -0.5

    def gain(k, shape):
        return 1.0 + 0.05 * jax.random.normal(k, shape, f32)

    A = jax.random.uniform(ks[8], (L, GDN_V_HEADS), f32, 1.0, 16.0)
    dt = jnp.exp(jax.random.uniform(ks[9], (L, GDN_V_HEADS), f32, math.log(1e-3), math.log(1e-1)))
    dt_bias = dt + jnp.log(-jnp.expm1(-dt))
    return {
        "x": jax.random.normal(ks[0], (BATCH, SEQ, D_MODEL), f32),
        "ffn1_norm": gain(ks[1], (L, D_MODEL)),
        "ffn1_w_in": dense(ks[2], (L, D_MODEL, 2 * D_FF)),
        "ffn1_w_out": dense(ks[3], (L, D_FF, D_MODEL)),
        "mix_norm": gain(ks[4], (L, D_MODEL)),
        "w_in": dense(ks[5], (L, D_MODEL, IN_WIDTH)),
        "hgrn_lb_logits": 0.5 * jax.random.normal(ks[6], (L + 1, HG_WIDTH_K), f32),
        "hgrn_out_norm": gain(ks[7], (L, HG_DV)),
        "gdn_conv_w": 0.5 * jax.random.normal(ks[10], (L, CONV_K, 2 * GDN_WIDTH_K + GDN_WIDTH_V), f32),
        "gdn_a_log": jnp.log(A),
        "gdn_dt_bias": dt_bias,
        "gdn_out_norm": gain(ks[11], (L, GDN_DV)),
        "w_branch_hgrn": dense(ks[12], (L, HG_WIDTH_V, D_MODEL)),
        "w_branch_gdn": dense(ks[13], (L, GDN_WIDTH_V, D_MODEL)),
        "w_out": dense(ks[14], (L, D_MODEL, D_MODEL)),
        "ffn2_norm": gain(ks[15], (L, D_MODEL)),
        "ffn2_w_in": dense(ks[16], (L, D_MODEL, 2 * D_FF)),
        "ffn2_w_out": dense(ks[17], (L, D_FF, D_MODEL)),
        "final_norm": gain(ks[18], (D_MODEL,)),
    }

def second_block(x, ffn1_norm, ffn1_w_in, ffn1_w_out, mix_norm, w_in, hgrn_lb_logits,
              hgrn_out_norm, gdn_conv_w, gdn_a_log, gdn_dt_bias, gdn_out_norm,
              w_branch_hgrn, w_branch_gdn, w_out, ffn2_norm, ffn2_w_in, ffn2_w_out,
              final_norm):
    lb_all = jnp.cumsum(jax.nn.softmax(hgrn_lb_logits.astype(jnp.float32), axis=0), axis=0)
    h = x
    for l in range(DEPTH_2):
        h = h + 0.5 * swiglu(rmsnorm(h, ffn1_norm[l]), ffn1_w_in[l], ffn1_w_out[l])
        h = h + hybrid_mixer(rmsnorm(h, mix_norm[l]), w_in[l], lb_all[l], hgrn_out_norm[l],
                             gdn_conv_w[l], gdn_a_log[l], gdn_dt_bias[l], gdn_out_norm[l],
                             w_branch_hgrn[l], w_branch_gdn[l], w_out[l])
        h = h + 0.5 * swiglu(rmsnorm(h, ffn2_norm[l]), ffn2_w_in[l], ffn2_w_out[l])
    return rmsnorm(h, final_norm)


def setup_inputs(seed=0):
    out = dict(first_inputs(seed))
    for name, value in second_inputs(seed + 1).items():
        if name != "x":
            out[name + "_2"] = value
    return out


def reference(
    x, positions, pre_norm, post_norm, w_in_even, w_out_even, w_in_odd, diff_lambda, diff_subln,
    mla_q_norm, mla_kv_norm, mla_w_uq, mla_w_ukv, w_out_odd, ffn1_norm_2, ffn1_w_in_2,
    ffn1_w_out_2, mix_norm_2, w_in_2, hgrn_lb_logits_2, hgrn_out_norm_2, gdn_conv_w_2,
    gdn_a_log_2, gdn_dt_bias_2, gdn_out_norm_2, w_branch_hgrn_2, w_branch_gdn_2, w_out_2,
    ffn2_norm_2, ffn2_w_in_2, ffn2_w_out_2, final_norm_2,
):
    x = first_block(
        x, positions, pre_norm, post_norm, w_in_even, w_out_even, w_in_odd, diff_lambda,
        diff_subln, mla_q_norm, mla_kv_norm, mla_w_uq, mla_w_ukv, w_out_odd,
    )
    return second_block(
        x, ffn1_norm_2, ffn1_w_in_2, ffn1_w_out_2, mix_norm_2, w_in_2, hgrn_lb_logits_2,
        hgrn_out_norm_2, gdn_conv_w_2, gdn_a_log_2, gdn_dt_bias_2, gdn_out_norm_2,
        w_branch_hgrn_2, w_branch_gdn_2, w_out_2, ffn2_norm_2, ffn2_w_in_2, ffn2_w_out_2,
        final_norm_2,
    )


_drawn_inputs = setup_inputs


def setup_inputs(seed=0):
    import zlib

    import numpy as np

    out = dict(_drawn_inputs(seed))
    spreads = {}
    factors = {'diff_subln': 24.474,
     'mla_q_norm': 8.0,
     'mla_kv_norm': 8.0,
     'ffn1_norm_2': 4.303,
     'mix_norm_2': 2.78,
     'hgrn_lb_logits_2': 5.255,
     'hgrn_out_norm_2': 6.952,
     'gdn_out_norm_2': 5.898,
     'ffn2_norm_2': 4.919}
    for name, (base, spread) in spreads.items():
        noise = np.random.default_rng([zlib.crc32(name.encode()), seed]).standard_normal(out[name].shape)
        drawn = base * np.exp(spread * noise) if base else spread * noise
        out[name] = __import__('jax').numpy.asarray(drawn.astype(out[name].dtype))
    for name, factor in factors.items():
        out[name] = (out[name] * factor).astype(out[name].dtype)
    return out
```

```python
from contextlib import ExitStack

import numpy as np

import concourse.bass as bass
from concourse import mybir

F32 = mybir.dt.float32
I32 = mybir.dt.int32
ALU = mybir.AluOpType
ACT = mybir.ActivationFunctionType
AX = mybir.AxisListType

P = 128
T = 512
NT = T // P
D = 1024
KD = D // P
BANK = 512
BANKS = 8
SLOTS = 2
EPS = 1e-6

A_H, A_D = 8, 64
I_H, I_D = 4, 64
TOPK = min(256, T // 4)
B_H, B_K, B_V = 4, 64, 128
EV = dict(aq=0, ak=512, av=1024, ag=1536, iq=2048, ik=2304, iw=2368, bq=2372, bk=2628, bv=2884, bg=3396)
C_H, C_K, C_V = 4, 64, 128
M_H, M_N, M_R, M_V = 8, 64, 32, 64
M_QL, M_KL = 256, 128
M_Q = M_N + M_R
OD = dict(cq=0, ck=512, cv=1024, cg=1536, dc=2048, dg=2464)
LAM_INIT = 0.8 - 0.6 * float(np.exp(-0.3))
D_FF = 2816
FT = D_FF // P
CH = 64
H_H = 8
G_QH, G_VH = 8, 16
MX = dict(hq=0, hf=1024, hi=2048, hg=3072, gq=4096, gk=5120, gv=6144, ga=8192, gb=8208, gz=8224,
          gate_h=10272, gate_g=11296)
LEVELS = 6

MASKED = -1.0e30
CAUSAL_OUT = -3.0e38
TAKEN = -3.4e38
IS_TAKEN = -3.3e38
LOWEST = -3.4e38


def constants():
    p = np.arange(P)
    s, t = p[:, None], p[None, :]
    same = (s // CH) == (t // CH)
    out = {}
    out["ident"] = (s == t)
    out["ones"] = np.ones((P, P))
    out["cum"] = (s <= t) & same
    u = np.arange(T)[None, :] - (T - P)
    out["causal"] = np.where(u <= s, 0.0, MASKED)
    out["causal_idx"] = np.where(u <= s, 0.0, CAUSAL_OUT)
    for lv in range(LEVELS):
        m = 1 << lv
        out[f"level{lv}"] = (s // (2 * m) == t // (2 * m)) & ((s // m) % 2 == 0) & ((t // m) % 2 == 1)
    gam = 1.0 - 2.0 ** (-5.0 - np.arange(B_H))
    for h in range(B_H):
        out[f"decay{h}"] = np.where(t >= s, gam[h] ** np.maximum(t - s, 0), 0.0)
    for pr in range(2):
        out[f"xi{pr}"] = gam[2 * pr + s // 64] ** (t + 1.0)
    out["zeta"] = gam[None, :] ** (P - 1.0 - s) * np.ones((P, B_H))
    out["gchunk"] = np.stack([gam[p // 64], gam[2 + p // 64]], 1) ** float(P)
    f32 = np.float32
    fb = f32(10000.0) ** (-np.arange(32, dtype=f32) / f32(32))
    fm = f32(10000.0) ** (-np.arange(16, dtype=f32) / f32(16))
    out["freq"] = np.ones((P, 1)) * np.concatenate([fb, fm])[None, :]
    out["scan"] = np.ones((P, 1)) * (np.arange(T)[None, :] % CH != 0)
    at, n = {}, 0
    for k, v in out.items():
        at[k] = (n, n + v.shape[1])
        n += v.shape[1]
    return np.concatenate([np.asarray(v, np.float32) for v in out.values()], 1), at


GAIN_ROWS = [("pre_norm", 16), ("ffn1_norm_2", 8), ("mix_norm_2", 8), ("ffn2_norm_2", 8),
             ("hgrn_lb_logits_2", 16), ("mla_q_norm", 2), ("mla_kv_norm", 1)]


def gain_at():
    at, n = {}, 0
    for k, c in GAIN_ROWS:
        at[k] = n
        n += c
    return at, n


def plan_weights(A, stages):
    blocks = []

    def cols(w, k0, k1, *pieces):
        src = w.rearrange("(k p) c -> p k c", p=P)
        blk, at = [], 0
        for c0, n in pieces:
            blk.append((at, src[:, k0:k1, c0:c0 + n]))
            at += n
        blocks.append(blk)

    def square(w, k_tiles=KD):
        for half in range(2):
            for k0 in range(0, k_tiles, KD):
                cols(w, k0, min(k0 + KD, k_tiles), (half * BANK, BANK))

    for stage in stages:
        if stage == "even":
            w = A["w_in_even"][0]
            for name in ("aq", "ak", "av", "ag"):
                cols(w, 0, KD, (EV[name], 512))
            cols(w, 0, KD, (EV["iq"], 256), (EV["ik"], 64), (EV["ik"], 64), (EV["iw"], 4))
            cols(w, 0, KD, (EV["bq"], 512))
            cols(w, 0, KD, (EV["bv"], 512))
            cols(w, 0, KD, (EV["bg"], 512))
            square(A["w_out_even"][0])
        if stage == "odd":
            w = A["w_in_odd"][0]
            for name in ("cq", "ck", "cv", "cg"):
                cols(w, 0, KD, (OD[name], 512))
            cols(w, 0, KD, (OD["dc"], M_QL + M_KL + M_R))
            cols(w, 0, KD, (OD["dg"], 512))
            blocks.append([(0, A["mla_w_uq"][0].rearrange("(k p) c -> p k c", p=P)[:, :, 0:512])])
            uq = A["mla_w_uq"][0].rearrange("(k p) c -> p k c", p=P)
            blocks[-1] = [("uq", uq), ("ukv", A["mla_w_ukv"][0])]
            square(A["w_out_odd"][0])
        if stage in ("ffn1", "ffn2"):
            w = A[f"{stage}_w_in_2"][0]
            for c in range(0, D_FF, 256):
                cols(w, 0, KD, (c, 256), (D_FF + c, 256))
            square(A[f"{stage}_w_out_2"][0], FT)
        if stage == "mix":
            w = A["w_in_2"][0]
            for g in range(2):
                for name in ("hf", "hq", "hi", "hg"):
                    cols(w, 0, KD, (MX[name] + 512 * g, 512))
            for half in range(2):
                cols(w, 0, KD, (MX["gate_h"] + 512 * half, 512))
            square(A["w_branch_hgrn_2"][0])
            cols(w, 0, KD, (MX["ga"], 32))
            for g in range(4):
                cols(w, 0, KD, (MX["gq"] + 256 * g, 256), (MX["gk"] + 256 * g, 256))
                cols(w, 0, KD, (MX["gv"] + 512 * g, 512))
                cols(w, 0, KD, (MX["gz"] + 512 * g, 512))
            for half in range(2):
                cols(w, 0, KD, (MX["gate_g"] + 512 * half, 512))
            square(A["w_branch_gdn_2"][0], 2 * KD)
            square(A["w_out_2"][0])
    return blocks


class Program:

    def __init__(self, nc, ctx, A, out, stages):
        self.nc, self.A, self.out, self.stages = nc, A, out, stages
        sb = lambda name, shape, dt=F32: ctx.enter_context(nc.sbuf_tensor(name, shape, dt))
        self.ctx = ctx
        self.x_res = sb("x_res", [P, NT, D])
        self.h_t = sb("h_t", [P, KD, T])
        self.ring = sb("weight_ring", [P, SLOTS, KD, BANK])
        n = A["consts"].shape[1]
        self.consts = sb("consts_sb", [P, n])
        _, self.const_at = constants()
        self.gains_at, self.n_gains = gain_at()
        self.gains = sb("gain_columns", [P, self.n_gains])
        self.conv_w = sb("conv_columns", [P, 4 * 32])
        self.row = sb("norm_row", [P, D])
        self.small_rows = sb("small_rows", [P, 3 * 128 + 32 + 256])
        self.stat = sb("statistics", [P, 512])
        self.ARENA = 30208
        self.arena = sb("arena", [P, self.ARENA])
        self.pos = sb("positions_sb", [P, NT], I32)
        self.psum = ctx.enter_context(nc.psum_tensor("psum", [P, BANKS, BANK], F32))
        sem = lambda name: ctx.enter_context(nc.semaphore(name))
        self.sem = sem
        self.bank_full = [sem(f"bank_full{i}") for i in range(BANKS)]
        self.bank_free = [sem(f"bank_free{i}") for i in range(BANKS)]
        self.weight_landed = [sem(f"weight_landed{i}") for i in range(SLOTS)]
        self.weights_used = sem("weights_used")
        self.consts_landed = sem("consts_landed")
        self.gain_rows_zeroed = sem("gain_rows_zeroed")
        self.row_landed = sem("row_landed")
        self.output_stored = sem("output_stored")
        self.phase_met = sem("phase_met")
        self.steps = {"dve": sem("dve_step"), "act": sem("act_step"), }
        self.step_n = {"dve": 0, "act": 0}
        self.angles_reduced = sem("angles_reduced")
        self.branches_added = sem("branches_added")
        self.conv_done = sem("conv_done")
        self.conv_silu = sem("conv_silu")
        self.end_scales = sem("end_scales")
        self.final_rows = sem("final_rows")
        self.gdn_decay = sem("gdn_decay")
        self.gdn_decays = sem("gdn_decays")
        self.gdn_diff = sem("gdn_diff")
        self.gdn_gated = sem("gdn_gated")
        self.group_deviations = sem("group_deviations")
        self.group_variances = sem("group_variances")
        self.head_squares = sem("head_squares")
        self.heads_normed = sem("heads_normed")
        self.heads_subtracted = sem("heads_subtracted")
        self.hgrn_decays = sem("hgrn_decays")
        self.hgrn_diffs = sem("hgrn_diffs")
        self.hgrn_end_decays = sem("hgrn_end_decays")
        self.hgrn_f = sem("hgrn_f")
        self.hgrn_factors = sem("hgrn_factors")
        self.hgrn_gated = sem("hgrn_gated")
        self.hgrn_k_to_end = sem("hgrn_k_to_end")
        self.hgrn_log_f = sem("hgrn_log_f")
        self.hgrn_squares = sem("hgrn_squares")
        self.gdn_squares = sem("gdn_squares")
        self.hgrn_states = sem("hgrn_states")
        self.hgrn_to_end = sem("hgrn_to_end")
        self.keys_whole = sem("keys_whole")
        self.kte_ready = sem("kte_ready")
        self.lambda_exps = sem("lambda_exps")
        self.lambda_sums = sem("lambda_sums")
        self.latent_squares = sem("latent_squares")
        self.latents_normed = sem("latents_normed")
        self.lb_exps = sem("lb_exps")
        self.lb_shifted = sem("lb_shifted")
        self.level_ready = sem("level_ready")
        self.probs_ready = sem("probs_ready")
        self.qe_ready = sem("qe_ready")
        self.qk_inverted = sem("qk_inverted")
        self.qk_squares = sem("qk_squares")
        self.queries_rotated = sem("queries_rotated")
        self.retention_states = sem("retention_states")
        self.rn_ready = sem("rn_ready")
        self.rotated = sem("rotated")
        self.row_used = sem("row_used")
        self.rows_normed = sem("rows_normed")
        self.rr_ready = sem("rr_ready")
        self.scores_masked = sem("scores_masked")
        self.softplus_exp = sem("softplus_exp")
        self.softplus_in = sem("softplus_in")
        self.softplus_ln = sem("softplus_ln")
        self.softplus_one = sem("softplus_one")
        self.squares_summed = sem("squares_summed")
        self.y_h_ready = sem("y_h_ready")
        self.y_h_wanted = sem("y_h_wanted")
        self.met = {}
        self.jobs = {}
        self.block_n = 0
        self.blocks = plan_weights(A, stages)
        self.landed_at = []
        count = [0] * SLOTS
        for i, blk in enumerate(self.blocks):
            count[i % SLOTS] += 16 * len(blk)
            self.landed_at.append(count[i % SLOTS])
        self.top = 0

    def const(self, name, n=None):
        a, b = self.const_at[name]
        return self.consts[:, a:b]

    def carve(self, at, *shape):
        n = int(np.prod(shape))
        assert at + n <= self.ARENA, (at, n)
        v = self.arena[:, at:at + n]
        if len(shape) == 2:
            v = v.rearrange("p (a b) -> p a b", b=shape[1])
        if len(shape) == 3:
            v = v.rearrange("p (a b c) -> p a b c", b=shape[1], c=shape[2])
        return v, at + n

    def next_bank(self, key):
        assert key not in self.jobs, key
        self.jobs[key] = len(self.jobs)
        return self.bank(key)

    def bank(self, key):
        return self.psum[:, self.jobs[key] % BANKS, :]

    def turn(self, key):
        return self.jobs[key] // BANKS + 1

    def full_of(self, key):
        return self.bank_full[self.jobs[key] % BANKS]

    def free_of(self, key):
        return self.bank_free[self.jobs[key] % BANKS]

    def one_more(self, who):
        self.step_n[who] += 1
        return self.steps[who]

    def phase_end(self, who):
        self.met[who] = self.met.get(who, 0) + 1
        return 3 * self.met[who]

    def next_block(self):
        self.block_n += 1
        return self.block_n - 1



def pe_transpose(K, pe, key, src, n_cols=P):
    bank = K.next_bank(key)
    if K.turn(key) > 1:
        pe.wait_ge(K.free_of(key), K.turn(key) - 1)
    for t in range(NT):
        last = pe.transpose(bank[0:n_cols, t * P:(t + 1) * P], src(t), K.const("ident"))
    last.then_inc(K.full_of(key), 1)


def pe_token_major(K, pe, key, act, n_cols, k0=0, nk=KD, col=0, blk=None, started=False, tiles=range(NT)):
    slot = K.ring[:, blk % SLOTS]
    for t in tiles:
        bank = K.next_bank((key, t))
        if K.turn((key, t)) > 1:
            pe.wait_ge(K.free_of((key, t)), K.turn((key, t)) - 1)
        for k in range(nk):
            last = pe.matmul(bank[:, 0:n_cols], act[:, k0 + k, t * P:(t + 1) * P], slot[:, k, col:col + n_cols],
                             start=(k == 0), stop=(k == nk - 1))
            if t == 0 and k == 0 and not started:
                last.then_inc(K.weights_used, 1)
        last.then_inc(K.full_of((key, t)), 1)


def pe_feature_major(K, pe, key, act, cols, blk, started=False):
    slot = K.ring[:, blk % SLOTS]
    for n, c in enumerate(cols):
        bank = K.next_bank((key, n))
        if K.turn((key, n)) > 1:
            pe.wait_ge(K.free_of((key, n)), K.turn((key, n)) - 1)
        for k in range(KD):
            last = pe.matmul(bank, slot[:, k, c:c + P], act[:, k, :], start=(k == 0), stop=(k == KD - 1))
            if n == 0 and k == 0 and not started:
                last.then_inc(K.weights_used, 1)
        last.then_inc(K.full_of((key, n)), 1)


def pe_square(K, pe, key, act, k_tiles=KD):
    for half in range(2):
        banks = []
        for t in range(NT):
            bank = K.next_bank((key, half, t))
            if K.turn((key, half, t)) > 1:
                pe.wait_ge(K.free_of((key, half, t)), K.turn((key, half, t)) - 1)
            banks.append(bank)
        for k0 in range(0, k_tiles, KD):
            blk = K.next_block()
            pe.wait_ge(K.weight_landed[blk % SLOTS], K.landed_at[blk])
            slot = K.ring[:, blk % SLOTS]
            nk = min(KD, k_tiles - k0)
            for t in range(NT):
                for k in range(nk):
                    last = pe.matmul(banks[t], act[:, k0 + k, t * P:(t + 1) * P], slot[:, k, :],
                                     start=(k0 + k == 0), stop=(k0 + k == k_tiles - 1))
                    if t == 0 and k == 0:
                        last.then_inc(K.weights_used, 1)
                if k0 + nk == k_tiles:
                    last.then_inc(K.full_of((key, half, t)), 1)


def pe_norm(K, pe, key, normed):
    for kt in range(KD):
        if kt == 0:
            pe.wait_ge(K.rows_normed, K.norm_n["pe"] + 1)
            K.norm_n["pe"] += 1
        pe_transpose(K, pe, (key, kt), lambda t, kt=kt: normed[:, t, kt * P:(kt + 1) * P])


def dve_norm(K, dve, src, normed, width=D):
    n = K.norm_n["dve"]
    K.norm_n["dve"] += 1
    ss = K.stat[:, 0:NT]
    dve.wait_ge(K.squares_summed, n + 1)
    dve.reciprocal(K.stat[:, 4:4 + NT], ss).then_inc(K.one_more("dve"), 1)
    dve.wait_ge(K.steps["dve"], K.step_n["dve"])
    for t in range(NT):
        ins = dve.tensor_scalar(normed[:, t, :], src[:, t, :], K.stat[:, 4 + t:5 + t], None, ALU.mult)
        if t < NT - 1:
            ins.then_inc(K.one_more("dve"), 1)
        else:
            ins.then_inc(K.rows_normed, 1)


def act_norm(K, act, src, junk):
    for t in range(NT):
        act.activation(junk[:, t, :], src[:, t, :], ACT.Square, accum_out=K.stat[:, 8 + t:9 + t]).then_inc(K.one_more("act"), 1)
    act.wait_ge(K.steps["act"], K.step_n["act"])
    act.activation(K.stat[:, 0:NT], K.stat[:, 8:8 + NT], ACT.Sqrt, bias=K.eps[:, 0:1], scale=1.0 / D).then_inc(K.squares_summed, 1)


def act_norm_out(K, act, key, gain):
    for kt in range(KD):
        act.wait_ge(K.full_of((key, kt)), K.turn((key, kt)))
        bank = K.bank((key, kt))
        act.activation(K.h_t[:, kt, :], bank, ACT.Copy, scale=K.gains[:, gain + kt:gain + kt + 1]).then_inc(K.free_of((key, kt)), 1)
    act.wait_ge(K.free_of((key, KD - 1)), K.turn((key, KD - 1)))



def sp_setup(K, sp):
    sp.dma_start(K.consts[:], K.A["consts"]).then_inc(K.consts_landed, 16)
    sp.dma_start(K.x_res[:], K.A["x"][0].rearrange("(t p) d -> p t d", p=P)).then_inc(K.consts_landed, 16)
    sp.dma_start(K.pos[:], K.A["positions"][0].rearrange("(t p) -> p t", p=P),
                 allow_slow_non_contiguous=True).then_inc(K.consts_landed, 16)
    stage, _ = K.carve(0, 2, P)
    sp.wait_ge(K.gain_rows_zeroed, 1)
    for name, n in GAIN_ROWS:
        r = K.gains_at[name]
        src = K.A[name]
        src = src.rearrange("a (r c) -> (a r) c", c=P)
        sp.dma_start(stage[r:r + n, 0, :], src).then_inc(K.consts_landed, 16)
    sp.dma_start(stage[:, 1, :], K.A["gdn_conv_w_2"][0].rearrange("j (r c) -> (j r) c", c=P)).then_inc(K.consts_landed, 16)
    at = 0
    for name, n in (("diff_subln", 128), ("hgrn_out_norm_2", 128), ("gdn_out_norm_2", 128), ("gdn_a_log_2", 16),
                    ("gdn_dt_bias_2", 16)):
        sp.dma_start(K.small_rows[:, at:at + n], K.A[name][0:1, :].to_broadcast([P, n])).then_inc(K.consts_landed, 16)
        at += n
    lam = K.A["diff_lambda"].rearrange("a b c -> a (b c)")
    sp.dma_start(K.small_rows[:, at:at + 256], lam.to_broadcast([P, 256])).then_inc(K.consts_landed, 16)


CONST_DMAS = 3 + len(GAIN_ROWS) + 1 + 6


def pe_setup(K, pe):
    pe.wait_ge(K.consts_landed, 16 * CONST_DMAS)
    stage, _ = K.carve(0, 2, P)
    bank = K.next_bank("gains")
    if K.turn("gains") > 1:
        pe.wait_ge(K.free_of("gains"), K.turn("gains") - 1)
    pe.transpose(bank[:, 0:P], stage[:, 0, :], K.const("ident"))
    pe.transpose(bank[:, P:2 * P], stage[:, 1, :], K.const("ident")).then_inc(K.full_of("gains"), 1)
    pe.drain().then_inc(K.phase_met, 1)
    pe.wait_ge(K.phase_met, K.phase_end("pe"))


def act_setup(K, act):
    act.wait_ge(K.angles_reduced, 1)
    _, trig, _ = trig_views(K)
    act.activation(K.trig[:], trig, ACT.Sin).then_inc(K.one_more("act"), 1)
    act.wait_ge(K.lambda_sums, 1)
    act.activation(K.lam[:, 2:4], K.lam[:, 0:2], ACT.Exp).then_inc(K.lambda_exps, 1)
    act.drain().then_inc(K.phase_met, 1)
    act.wait_ge(K.phase_met, K.phase_end("act"))


def trig_views(K):
    ang, e = K.carve(256, NT, 48)
    red, e = K.carve(e, 2, NT * 48)
    tmp, e = K.carve(e, 2, NT * 48)
    return ang, red, tmp


def dve_setup(K, dve):
    stage, _ = K.carve(0, 2, P)
    dve.memset(K.stat[:], 0.0).then_inc(K.one_more("dve"), 1)
    dve.memset(K.eps[:], EPS).then_inc(K.one_more("dve"), 1)
    dve.wait_ge(K.steps["dve"], K.step_n["dve"])
    dve.memset(stage[:, 0, :], 0.0).then_inc(K.gain_rows_zeroed, 1)
    dve.wait_ge(K.consts_landed, 16 * CONST_DMAS)
    dve.wait_ge(K.full_of("gains"), K.turn("gains"))
    bank = K.bank("gains")
    dve.tensor_copy(K.gains[:], bank[:, 0:K.n_gains]).then_inc(K.one_more("dve"), 1)
    dve.wait_ge(K.steps["dve"], K.step_n["dve"])
    dve.tensor_copy(K.conv_w[:], bank[:, P:2 * P]).then_inc(K.free_of("gains"), 1)
    ang, red, tmp = trig_views(K)
    posf = K.stat[:, 0:NT]
    dve.tensor_copy(posf, K.pos[:]).then_inc(K.one_more("dve"), 1)
    dve.wait_ge(K.steps["dve"], K.step_n["dve"])
    for t in range(NT):
        dve.tensor_scalar(ang[:, t, :], K.const("freq"), posf[:, t:t + 1], None, ALU.mult).then_inc(K.one_more("dve"), 1)
    dve.wait_ge(K.steps["dve"], K.step_n["dve"])
    magic = 12582912.0
    flat = ang.rearrange("p a b -> p (a b)")
    two_pi = 2 * np.pi
    c1 = 6.28125
    c2 = float(np.float32(np.floor((two_pi - c1) * 2 ** 22) / 2 ** 22))
    c3 = two_pi - c1 - c2
    for n, quarter in ((0, 0.0), (1, 0.25)):
        dve.tensor_scalar(tmp[:, n, :], flat, 1.0 / two_pi, quarter, ALU.mult, ALU.add).then_inc(K.one_more("dve"), 1)
        dve.wait_ge(K.steps["dve"], K.step_n["dve"])
        dve.tensor_scalar(tmp[:, n, :], tmp[:, n, :], magic, None, ALU.add).then_inc(K.one_more("dve"), 1)
        dve.wait_ge(K.steps["dve"], K.step_n["dve"])
        dve.tensor_scalar(tmp[:, n, :], tmp[:, n, :], -magic, None, ALU.add).then_inc(K.one_more("dve"), 1)
        dve.wait_ge(K.steps["dve"], K.step_n["dve"])
        dve.scalar_tensor_tensor(red[:, n, :], tmp[:, n, :], -c1, flat, ALU.mult, ALU.add).then_inc(K.one_more("dve"), 1)
        dve.wait_ge(K.steps["dve"], K.step_n["dve"])
        dve.scalar_tensor_tensor(red[:, n, :], tmp[:, n, :], -c2, red[:, n, :], ALU.mult, ALU.add).then_inc(K.one_more("dve"), 1)
        dve.wait_ge(K.steps["dve"], K.step_n["dve"])
        dve.scalar_tensor_tensor(red[:, n, :], tmp[:, n, :], -c3, red[:, n, :], ALU.mult, ALU.add).then_inc(K.one_more("dve"), 1)
        dve.wait_ge(K.steps["dve"], K.step_n["dve"])
        dve.tensor_scalar(red[:, n, :], red[:, n, :], np.pi / 2 * n, 3.1415925, ALU.add, ALU.min).then_inc(K.one_more("dve"), 1)
        dve.wait_ge(K.steps["dve"], K.step_n["dve"])
        ins = dve.tensor_scalar(red[:, n, :], red[:, n, :], -3.1415925, None, ALU.max)
        if n == 0:
            ins.then_inc(K.one_more("dve"), 1)
            dve.wait_ge(K.steps["dve"], K.step_n["dve"])
        else:
            ins.then_inc(K.angles_reduced, 1)
    for n in range(2):
        a = K.small_rows[:, 416 + 128 * n:416 + 128 * n + 64]
        b = K.small_rows[:, 416 + 128 * n + 64:416 + 128 * (n + 1)]
        dve.tensor_tensor_reduce(out=tmp[:, 0, 0:64], in0=a, in1=b, scale=1.0, scalar=0.0,
                                                    op0=ALU.mult, op1=ALU.add, accum_out=K.lam[:, n:n + 1]).then_inc(K.one_more("dve"), 1)
        dve.wait_ge(K.steps["dve"], K.step_n["dve"])
    dve.tensor_copy(K.stat[:, 76:77], posf[:, 0:1]).then_inc(K.lambda_sums, 1)
    dve.wait_ge(K.lambda_exps, 1)
    dve.tensor_tensor(K.lam[:, 4:5], K.lam[:, 3:4], K.lam[:, 2:3], ALU.subtract).then_inc(K.one_more("dve"), 1)
    dve.wait_ge(K.steps["dve"], K.step_n["dve"])
    dve.tensor_scalar(K.lam[:, 4:5], K.lam[:, 4:5], -LAM_INIT, None, ALU.add).then_inc(K.one_more("dve"), 1)
    dve.wait_ge(K.steps["dve"], K.step_n["dve"])
    dve.drain().then_inc(K.phase_met, 1)
    dve.wait_ge(K.phase_met, K.phase_end("dve"))



FFN_BLOCKS = D_FF // 256


def ffn_views(K):
    g_t, e = K.carve(0, FT, T)
    silu_a, e = K.carve(e, 4, T)
    normed, _ = K.carve(0, NT, D)
    junk, _ = K.carve(NT * D, NT, D)
    return g_t, silu_a, normed, junk


def pe_ffn(K, pe, s):
    g_t, _, normed, _ = ffn_views(K)
    pe_norm(K, pe, (s, "norm"), normed)
    pe.drain().then_inc(K.phase_met, 1)
    pe.wait_ge(K.phase_met, K.phase_end("pe"))
    for b in range(FFN_BLOCKS):
        blk = K.next_block()
        pe.wait_ge(K.weight_landed[blk % SLOTS], K.landed_at[blk])
        pe_feature_major(K, pe, (s, b), K.h_t, [0, P, 2 * P, 3 * P], blk)
    for b in range(FFN_BLOCKS):
        for n in range(2):
            pe.wait_ge(K.free_of(((s, b), 2 + n)), K.turn(((s, b), 2 + n)))
    pe_square(K, pe, (s, "out"), g_t, FT)
    pe.drain().then_inc(K.phase_met, 1)
    pe.wait_ge(K.phase_met, K.phase_end("pe"))


def act_ffn(K, act, s):
    _, silu_a, normed, junk = ffn_views(K)
    act_norm(K, act, K.x_res, junk)
    act_norm_out(K, act, (s, "norm"), K.gains_at[f"{s}_norm_2"])
    act.drain().then_inc(K.phase_met, 1)
    act.wait_ge(K.phase_met, K.phase_end("act"))
    for b in range(FFN_BLOCKS):
        for n in range(2):
            act.wait_ge(K.full_of(((s, b), n)), K.turn(((s, b), n)))
            a = K.bank(((s, b), n))
            if b >= 2:
                act.wait_ge(K.free_of(((s, b - 2), 2 + n)), K.turn(((s, b - 2), 2 + n)))
            act.activation(silu_a[:, 2 * (b % 2) + n, :], a, ACT.Silu).then_inc(K.free_of(((s, b), n)), 1)
    act.drain().then_inc(K.phase_met, 1)
    act.wait_ge(K.phase_met, K.phase_end("act"))


def dve_ffn(K, dve, s):
    g_t, silu_a, normed, _ = ffn_views(K)
    dve_norm(K, dve, K.x_res, normed)
    dve.drain().then_inc(K.phase_met, 1)
    dve.wait_ge(K.phase_met, K.phase_end("dve"))
    for b in range(FFN_BLOCKS):
        for n in range(2):
            dve.wait_ge(K.full_of(((s, b), 2 + n)), K.turn(((s, b), 2 + n)))
            up = K.bank(((s, b), 2 + n))
            dve.wait_ge(K.free_of(((s, b), n)), K.turn(((s, b), n)))
            dve.tensor_tensor(g_t[:, 2 * b + n, :], silu_a[:, 2 * (b % 2) + n, :], up, ALU.mult).then_inc(K.free_of(((s, b), 2 + n)), 1)
    for half in range(2):
        for t in range(NT):
            dve.wait_ge(K.full_of(((s, "out"), half, t)), K.turn(((s, "out"), half, t)))
            o = K.bank(((s, "out"), half, t))
            x = K.x_res[:, t, half * BANK:(half + 1) * BANK]
            dve.scalar_tensor_tensor(x, o, 0.5, x, ALU.mult, ALU.add).then_inc(K.free_of(((s, "out"), half, t)), 1)
    dve.drain().then_inc(K.phase_met, 1)
    dve.wait_ge(K.phase_met, K.phase_end("dve"))

def over(ap, n, axis=1):
    shape = list(ap.shape)
    shape.insert(axis, n)
    return ap.unsqueeze(axis).to_broadcast(shape)


def attention_buffers(K, at):
    masked, at = K.carve(at, 2, T)
    probs, at = K.carve(at, 2, T)
    probs_t, at = K.carve(at, 2, T)
    return masked, probs, probs_t, at




def pe_attention(K, pe, tag, steps, bufs):
    _, probs, probs_t = bufs
    n_steps, base = len(steps), K.att_base[tag]
    for m in range(n_steps + 2):
        if m < n_steps:
            q, k = steps[m]["q"], steps[m]["k"]
            bank = K.next_bank((tag, "s", m))
            if K.turn((tag, "s", m)) > 1:
                pe.wait_ge(K.free_of((tag, "s", m)), K.turn((tag, "s", m)) - 1)
            pe.matmul(bank[:, 0:k.shape[-1]], q, k, start=True, stop=True).then_inc(K.full_of((tag, "s", m)), 1)
        if 1 <= m <= n_steps:
            i = m - 1
            pe.wait_ge(K.probs_ready, base + i + 1)
            bank = K.next_bank((tag, "t", i))
            if K.turn((tag, "t", i)) > 1:
                pe.wait_ge(K.free_of((tag, "t", i)), K.turn((tag, "t", i)) - 1)
            for kb in range(steps[i]["k"].shape[-1] // P):
                last = pe.transpose(bank[:, kb * P:(kb + 1) * P], probs[:, i % 2, kb * P:(kb + 1) * P],
                                    K.const("ident"))
            last.then_inc(K.full_of((tag, "t", i)), 1)
        if m >= 2:
            i = m - 2
            pe.wait_ge(K.free_of((tag, "t", i)), K.turn((tag, "t", i)))
            bank = K.next_bank((tag, "o", i))
            if K.turn((tag, "o", i)) > 1:
                pe.wait_ge(K.free_of((tag, "o", i)), K.turn((tag, "o", i)) - 1)
            nkb = steps[i]["k"].shape[-1] // P
            for kb in range(nkb):
                v = steps[i]["v"](kb)
                last = pe.matmul(bank[:, 0:v.shape[-1]], probs_t[:, i % 2, kb * P:(kb + 1) * P], v,
                                 start=(kb == 0), stop=(kb == nkb - 1))
            last.then_inc(K.full_of((tag, "o", i)), 1)


def act_attention(K, act, tag, steps, bufs):
    masked, probs, probs_t = bufs
    n_steps, base = len(steps), K.att_base[tag]
    for n in range(n_steps + 1):
        if n < n_steps:
            nk = steps[n]["k"].shape[-1]
            act.wait_ge(K.scores_masked, base + n + 1)
            if n >= 2:
                act.wait_ge(K.full_of((tag, "t", n - 2)), K.turn((tag, "t", n - 2)))
            act.activation(probs[:, n % 2, 0:nk], masked[:, n % 2, 0:nk], ACT.Exp,
                                  bias=K.stat[:, 20 + n % 4:21 + n % 4], scale=steps[n]["scale"],
                                  accum_out=K.stat[:, 24 + n % 8:25 + n % 8]).then_inc(K.probs_ready, 1)
        if n >= 1:
            i = n - 1
            nk = steps[i]["k"].shape[-1]
            act.wait_ge(K.full_of((tag, "t", i)), K.turn((tag, "t", i)))
            bank = K.bank((tag, "t", i))
            if i >= 2:
                act.wait_ge(K.full_of((tag, "o", i - 2)), K.turn((tag, "o", i - 2)))
            act.copy(probs_t[:, i % 2, 0:nk], bank[:, 0:nk]).then_inc(K.free_of((tag, "t", i)), 1)


def dve_attention(K, dve, tag, steps, bufs):
    masked, _, _ = bufs
    n_steps, base = len(steps), K.att_base[tag]
    for n in range(n_steps + 3):
        if n < n_steps:
            nk = steps[n]["k"].shape[-1]
            dve.wait_ge(K.full_of((tag, "s", n)), K.turn((tag, "s", n)))
            bank = K.bank((tag, "s", n))
            if n >= 2:
                dve.wait_ge(K.probs_ready, base + n - 1)
            dve.tensor_tensor_reduce(
                out=masked[:, n % 2, 0:nk], in0=bank[:, 0:nk], in1=steps[n]["bias"], scale=1.0, scalar=LOWEST,
                op0=ALU.add, op1=ALU.max, accum_out=K.stat[:, 16 + n % 4:17 + n % 4]).then_inc(K.free_of((tag, "s", n)), 1)
            dve.wait_ge(K.free_of((tag, "s", n)), K.turn((tag, "s", n)))
            dve.tensor_scalar(K.stat[:, 20 + n % 4:21 + n % 4], K.stat[:, 16 + n % 4:17 + n % 4],
                                     -steps[n]["scale"], None, ALU.mult).then_inc(K.scores_masked, 1)
        if n >= 3:
            i = n - 3
            dve.wait_ge(K.probs_ready, base + i + 1)
            dve.reciprocal(K.stat[:, 32 + i % 8:33 + i % 8], K.stat[:, 24 + i % 8:25 + i % 8]).then_inc(K.one_more("dve"), 1)
            dve.wait_ge(K.steps["dve"], K.step_n["dve"])
            dve.wait_ge(K.full_of((tag, "o", i)), K.turn((tag, "o", i)))
            bank = K.bank((tag, "o", i))
            out = steps[i]["out"]
            dve.tensor_scalar(out, bank[:, 0:out.shape[-1]], K.stat[:, 32 + i % 8:33 + i % 8], None,
                                     ALU.mult).then_inc(K.free_of((tag, "o", i)), 1)
    dve.wait_ge(K.free_of((tag, "o", n_steps - 1)), K.turn((tag, "o", n_steps - 1)))



def pe_mix_out(K, pe, s, mixed):
    for kt in range(KD):
        pe_transpose(K, pe, (s, "mixed", kt), lambda t, kt=kt: mixed[:, t, kt * P:(kt + 1) * P])
    pe.wait_ge(K.free_of((s, "mixed", KD - 1)), K.turn((s, "mixed", KD - 1)))
    pe_square(K, pe, (s, "out"), K.h_t)


def act_mix_out(K, act, s, proj, junk):
    for kt in range(KD):
        act.wait_ge(K.full_of((s, "mixed", kt)), K.turn((s, "mixed", kt)))
        bank = K.bank((s, "mixed", kt))
        if kt:
            act.wait_ge(K.free_of((s, "mixed", kt - 1)), K.turn((s, "mixed", kt - 1)))
        act.copy(K.h_t[:, kt, :], bank).then_inc(K.free_of((s, "mixed", kt)), 1)
    for half in range(2):
        for t in range(NT):
            act.wait_ge(K.full_of(((s, "out"), half, t)), K.turn(((s, "out"), half, t)))
            bank = K.bank(((s, "out"), half, t))
            act.copy(proj[:, t, half * BANK:(half + 1) * BANK], bank).then_inc(K.free_of(((s, "out"), half, t)), 1)
    for t in range(NT):
        act.wait_ge(K.free_of(((s, "out"), 1, t)), K.turn(((s, "out"), 1, t)))
    act_norm(K, act, proj, junk)


def dve_mix_out(K, dve, s, proj):
    n = K.norm_n["dve"]
    K.norm_n["dve"] += 1
    K.norm_n["pe"] += 1
    dve.wait_ge(K.squares_summed, n + 1)
    dve.reciprocal(K.stat[:, 4:4 + NT], K.stat[:, 0:NT]).then_inc(K.one_more("dve"), 1)
    dve.wait_ge(K.steps["dve"], K.step_n["dve"])
    K.rows_landed += 16
    dve.wait_ge(K.row_landed, K.rows_landed)
    for t in range(NT):
        ins = dve.scalar_tensor_tensor(proj[:, t, :], proj[:, t, :], K.stat[:, 4 + t:5 + t], K.row[:],
                                       ALU.mult, ALU.mult)
        if t < NT - 1:
            ins.then_inc(K.one_more("dve"), 1)
        else:
            ins.then_inc(K.row_used, 1)
            K.rows_used += 1
            dve.wait_ge(K.row_used, K.rows_used)
    for t in range(NT):
        dve.tensor_tensor(K.x_res[:, t, :], K.x_res[:, t, :], proj[:, t, :], ALU.add).then_inc(K.one_more("dve"), 1)



def even_views(K):
    V, e = {}, 0
    for name, shape in (("aq_t", (4, T)), ("ak_t", (4, T)), ("av", (NT, 512)), ("ag", (NT, 512)), ("iq_t", (2, T)),
                        ("ik_t", (1, T)), ("iw", (NT, 4)), ("bqk", (NT, 512)), ("bv", (NT, 512)),
                        ("bg", (NT, 512)), ("mixed", (NT, D)), ("select", (NT - 1, T))):
        V[name], e = K.carve(e, *shape)
    V["att"] = attention_buffers(K, e)[:3]
    V["work"], e2 = K.carve(e, 2, T)
    V["tmp"], e2 = K.carve(e2, 1, T)
    V["top8"], e2 = K.carve(e2, 1, 8)
    e = 0
    for name, shape in (("rot", (NT, 512)), ("qk_t", (4, T)), ("qx_t", (2, T)), ("kz", (NT, 256)),
                        ("sd_t", (NT * B_H, P))):
        V[name], e = K.carve(e, *shape)
    assert e <= 8192
    V["state"], _ = K.carve(8192, 2 * NT, P)
    V["rot_tmp"], _ = K.carve(21520, 4, 256)
    V["proj"], e = K.carve(0, NT, D)
    V["junk"], e = K.carve(e, NT, D)
    V["normed"], _ = K.carve(0, NT, D)
    return V


def even_steps(K, V):
    steps = []
    for h in range(A_H):
        p, ct = 64 * (h % 2), h // 2
        for i in range(NT):
            nk = (i + 1) * P
            steps.append(dict(q=V["aq_t"][p:p + 64, ct, i * P:nk], k=V["ak_t"][p:p + 64, ct, 0:nk],
                              v=lambda kb, h=h: V["av"][:, kb, h * 64:(h + 1) * 64],
                              bias=V["select"][:, i - 1, 0:nk] if i else K.const("causal")[:, T - nk:T],
                              scale=A_D ** -0.5, out=V["mixed"][:, i, h * 64:(h + 1) * 64]))
    return steps


def pe_even(K, pe, s):
    V = even_views(K)
    pe_norm(K, pe, (s, "norm"), V["normed"])
    pe.drain().then_inc(K.phase_met, 1)
    pe.wait_ge(K.phase_met, K.phase_end("pe"))
    for name in ("aq", "ak"):
        blk = K.next_block()
        pe.wait_ge(K.weight_landed[blk % SLOTS], K.landed_at[blk])
        pe_feature_major(K, pe, (s, name), K.h_t, [0, P, 2 * P, 3 * P], blk)
    for name in ("av", "ag"):
        blk = K.next_block()
        pe.wait_ge(K.weight_landed[blk % SLOTS], K.landed_at[blk])
        pe_token_major(K, pe, (s, name), K.h_t, 512, blk=blk)
    blk = K.next_block()
    pe.wait_ge(K.weight_landed[blk % SLOTS], K.landed_at[blk])
    pe_feature_major(K, pe, (s, "i"), K.h_t, [0, P, 2 * P], blk)
    pe_token_major(K, pe, (s, "iw"), K.h_t, 4, col=384, blk=blk, started=True)
    pe.drain().then_inc(K.phase_met, 1)
    pe.wait_ge(K.phase_met, K.phase_end("pe"))
    for i in range(1, NT):
        nk = (i + 1) * P
        for h in range(I_H):
            p = 64 * (h % 2)
            bank = K.next_bank((s, "index", i, h))
            if K.turn((s, "index", i, h)) > 1:
                pe.wait_ge(K.free_of((s, "index", i, h)), K.turn((s, "index", i, h)) - 1)
            pe.matmul(bank[:, 0:nk], V["iq_t"][p:p + 64, h // 2, i * P:nk], V["ik_t"][p:p + 64, 0, 0:nk],
                               start=True, stop=True).then_inc(K.full_of((s, "index", i, h)), 1)
        name = ("bqk", "bv", "bg")[i - 1]
        blk = K.next_block()
        pe.wait_ge(K.weight_landed[blk % SLOTS], K.landed_at[blk])
        pe_token_major(K, pe, (s, name), K.h_t, 512, blk=blk)
    pe.drain().then_inc(K.phase_met, 1)
    pe.wait_ge(K.phase_met, K.phase_end("pe"))
    pe_attention(K, pe, "a", even_steps(K, V), V["att"])
    pe.drain().then_inc(K.phase_met, 1)
    pe.wait_ge(K.phase_met, K.phase_end("pe"))
    pe.wait_ge(K.rotated, 1)
    for c in range(4):
        pe_transpose(K, pe, (s, "rot", c), lambda t, c=c: V["rot"][:, t, c * P:(c + 1) * P])
    for t in range(NT):
        bank = K.next_bank((s, "u", t))
        if K.turn((s, "u", t)) > 1:
            pe.wait_ge(K.free_of((s, "u", t)), K.turn((s, "u", t)) - 1)
        for h in range(B_H):
            p = 64 * (h % 2)
            last = pe.matmul(bank[p:p + 64, (h // 2) * P:(h // 2 + 1) * P], V["kz"][:, t, h * 64:(h + 1) * 64],
                             V["bv"][:, t, h * P:(h + 1) * P], start=True, stop=True)
        last.then_inc(K.full_of((s, "u", t)), 1)
    pe.wait_ge(K.free_of((s, "rot", 3)), K.turn((s, "rot", 3)))
    for t in range(NT):
        ts = slice(t * P, (t + 1) * P)
        for par in range(2):
            p = 64 * par
            bank = K.next_bank((s, "qk", t, par))
            if K.turn((s, "qk", t, par)) > 1:
                pe.wait_ge(K.free_of((s, "qk", t, par)), K.turn((s, "qk", t, par)) - 1)
            for c in range(2):
                last = pe.matmul(bank[:, c * P:(c + 1) * P], V["qk_t"][p:p + 64, 2 + c, ts],
                                 V["qk_t"][p:p + 64, c, ts], start=True, stop=True)
            last.then_inc(K.full_of((s, "qk", t, par)), 1)
    pe.wait_ge(K.retention_states, 1)
    for t in range(NT):
        for par in range(2):
            pe.wait_ge(K.free_of((s, "qk", t, par)), K.turn((s, "qk", t, par)))
        for par in range(2):
            p = 64 * par
            bank = K.next_bank((s, "r", t, par))
            if K.turn((s, "r", t, par)) > 1:
                pe.wait_ge(K.free_of((s, "r", t, par)), K.turn((s, "r", t, par)) - 1)
            for c in range(2):
                h, o = 2 * c + par, bank[:, c * P:(c + 1) * P]
                last = pe.matmul(o, V["sd_t"][:, t * B_H + h, :], V["bv"][:, t, h * P:(h + 1) * P],
                                 start=True, stop=(t == 0))
                if t:
                    last = pe.matmul(o, V["qx_t"][p:p + 64, c, t * P:(t + 1) * P],
                                     V["state"][p:p + 64, c * NT + t, :], start=False, stop=True)
            last.then_inc(K.full_of((s, "r", t, par)), 1)
    pe.drain().then_inc(K.phase_met, 1)
    pe.wait_ge(K.phase_met, K.phase_end("pe"))
    pe_mix_out(K, pe, s, V["mixed"])
    pe.drain().then_inc(K.phase_met, 1)
    pe.wait_ge(K.phase_met, K.phase_end("pe"))


def act_even(K, act, s):
    V = even_views(K)
    act_norm(K, act, K.x_res, V["junk"])
    act_norm_out(K, act, (s, "norm"), K.gains_at["pre_norm"])
    act.drain().then_inc(K.phase_met, 1)
    act.wait_ge(K.phase_met, K.phase_end("act"))
    for name, dst in (("aq", "aq_t"), ("ak", "ak_t")):
        for c in range(4):
            act.wait_ge(K.full_of(((s, name), c)), K.turn(((s, name), c)))
            act.copy(V[dst][:, c, :], K.bank(((s, name), c))).then_inc(K.free_of(((s, name), c)), 1)
    for t in range(NT):
        act.wait_ge(K.full_of(((s, "av"), t)), K.turn(((s, "av"), t)))
        act.copy(V["av"][:, t, :], K.bank(((s, "av"), t))).then_inc(K.free_of(((s, "av"), t)), 1)
    for t in range(NT):
        act.wait_ge(K.full_of(((s, "ag"), t)), K.turn(((s, "ag"), t)))
        act.activation(V["ag"][:, t, :], K.bank(((s, "ag"), t)), ACT.Silu).then_inc(K.free_of(((s, "ag"), t)), 1)
    for c in range(3):
        dst = V["iq_t"][:, c, :] if c < 2 else V["ik_t"][:, 0, :]
        act.wait_ge(K.full_of(((s, "i"), c)), K.turn(((s, "i"), c)))
        act.copy(dst, K.bank(((s, "i"), c))).then_inc(K.free_of(((s, "i"), c)), 1)
    for t in range(NT):
        act.wait_ge(K.full_of(((s, "iw"), t)), K.turn(((s, "iw"), t)))
        act.activation(V["iw"][:, t, :], K.bank(((s, "iw"), t))[:, 0:4], ACT.Copy,
                              scale=I_H ** -0.5 * I_D ** -0.5).then_inc(K.free_of(((s, "iw"), t)), 1)
    act.drain().then_inc(K.phase_met, 1)
    act.wait_ge(K.phase_met, K.phase_end("act"))
    for name in ("bqk", "bv"):
        for t in range(NT):
            act.wait_ge(K.full_of(((s, name), t)), K.turn(((s, name), t)))
            act.copy(V[name][:, t, :], K.bank(((s, name), t))).then_inc(K.free_of(((s, name), t)), 1)
    for t in range(NT):
        act.wait_ge(K.full_of(((s, "bg"), t)), K.turn(((s, "bg"), t)))
        act.activation(V["bg"][:, t, :], K.bank(((s, "bg"), t)), ACT.Silu).then_inc(K.free_of(((s, "bg"), t)), 1)
    act.drain().then_inc(K.phase_met, 1)
    act.wait_ge(K.phase_met, K.phase_end("act"))
    act_attention(K, act, "a", even_steps(K, V), V["att"])
    act.drain().then_inc(K.phase_met, 1)
    act.wait_ge(K.phase_met, K.phase_end("act"))
    for c in range(4):
        act.wait_ge(K.full_of((s, "rot", c)), K.turn((s, "rot", c)))
        act.copy(V["qk_t"][:, c, :], K.bank((s, "rot", c))).then_inc(K.free_of((s, "rot", c)), 1)
        act.wait_ge(K.free_of((s, "rot", c)), K.turn((s, "rot", c)))
    for t in range(NT):
        heads = V["mixed"][:, t, 512:1024].rearrange("p (c r e) -> p c r e", c=2, r=2)
        for par in range(2):
            act.wait_ge(K.full_of((s, "r", t, par)), K.turn((s, "r", t, par)))
            src = K.bank((s, "r", t, par))[:, 0:256].rearrange("p (c e) -> p c e", c=2)
            act.copy(heads[:, :, par, :], src).then_inc(K.free_of((s, "r", t, par)), 1)
    act.wait_ge(K.group_variances, 1)
    act.activation(K.stat[:, 96:112], K.stat[:, 80:96], ACT.Sqrt, bias=K.eps[:, 0:1]).then_inc(K.group_deviations, 1)
    act.drain().then_inc(K.phase_met, 1)
    act.wait_ge(K.phase_met, K.phase_end("act"))
    act_mix_out(K, act, s, V["proj"], V["junk"])
    act.drain().then_inc(K.phase_met, 1)
    act.wait_ge(K.phase_met, K.phase_end("act"))


def dve_rotate(K, dve, src, dst, n_heads, half, freq0, t, tmp):
    x1 = src[:, :, 0:half]
    x2 = src[:, :, half:2 * half]
    sin = over(K.trig[:, 0, t * 48 + freq0:t * 48 + freq0 + half], n_heads)
    cos = over(K.trig[:, 1, t * 48 + freq0:t * 48 + freq0 + half], n_heads)
    w = [tmp[:, i, 0:n_heads * half].rearrange("p (h c) -> p h c", h=n_heads) for i in range(4)]
    dve.tensor_tensor(w[0], x1, cos, ALU.mult).then_inc(K.one_more("dve"), 1)
    dve.tensor_tensor(w[1], x2, sin, ALU.mult).then_inc(K.one_more("dve"), 1)
    dve.tensor_tensor(w[2], x1, sin, ALU.mult).then_inc(K.one_more("dve"), 1)
    dve.tensor_tensor(w[3], x2, cos, ALU.mult).then_inc(K.one_more("dve"), 1)
    dve.wait_ge(K.steps["dve"], K.step_n["dve"])
    dve.tensor_tensor(dst[:, :, 0:half], w[0], w[1], ALU.subtract).then_inc(K.one_more("dve"), 1)
    dve.tensor_tensor(dst[:, :, half:2 * half], w[2], w[3], ALU.add).then_inc(K.one_more("dve"), 1)
    dve.wait_ge(K.steps["dve"], K.step_n["dve"])


def dve_even(K, dve, s):
    V = even_views(K)
    dve_norm(K, dve, K.x_res, V["normed"])
    dve.drain().then_inc(K.phase_met, 1)
    dve.wait_ge(K.phase_met, K.phase_end("dve"))
    dve.drain().then_inc(K.phase_met, 1)
    dve.wait_ge(K.phase_met, K.phase_end("dve"))
    work, tmp, top8 = V["work"], V["tmp"][:, 0], V["top8"][:, 0]
    for i in range(1, NT):
        nk = (i + 1) * P
        for h in range(I_H):
            key = (s, "index", i, h)
            dve.wait_ge(K.full_of(key), K.turn(key))
            bank = K.bank(key)
            dst = work[:, 0, 0:nk] if h == 0 else tmp[:, 0:nk]
            dve.tensor_scalar(dst, bank[:, 0:nk], 0.0, V["iw"][:, i, h:h + 1], ALU.max, ALU.mult).then_inc(K.free_of(key), 1)
            dve.wait_ge(K.free_of(key), K.turn(key))
            if h:
                dve.tensor_tensor(work[:, 0, 0:nk], work[:, 0, 0:nk], dst, ALU.add).then_inc(K.one_more("dve"), 1)
                dve.wait_ge(K.steps["dve"], K.step_n["dve"])
        dve.tensor_tensor(work[:, 0, 0:nk], work[:, 0, 0:nk], K.const("causal_idx")[:, T - nk:T],
                                             ALU.add).then_inc(K.one_more("dve"), 1)
        dve.wait_ge(K.steps["dve"], K.step_n["dve"])
        for r in range(TOPK // 8):
            a, b = work[:, r % 2, 0:nk], work[:, (r + 1) % 2, 0:nk]
            dve.max(top8, a).then_inc(K.one_more("dve"), 1)
            dve.wait_ge(K.steps["dve"], K.step_n["dve"])
            dve.match_replace(b, top8, a, TAKEN).then_inc(K.one_more("dve"), 1)
            dve.wait_ge(K.steps["dve"], K.step_n["dve"])
        dve.tensor_scalar(V["select"][:, i - 1, 0:nk], work[:, (TOPK // 8) % 2, 0:nk], IS_TAKEN,
                                             MASKED, ALU.is_ge, ALU.mult).then_inc(K.one_more("dve"), 1)
        dve.wait_ge(K.steps["dve"], K.step_n["dve"])
    dve.drain().then_inc(K.phase_met, 1)
    dve.wait_ge(K.phase_met, K.phase_end("dve"))
    dve_attention(K, dve, "a", even_steps(K, V), V["att"])
    for t in range(NT):
        m = V["mixed"][:, t, 0:512]
        dve.tensor_tensor(m, m, V["ag"][:, t, :], ALU.mult).then_inc(K.one_more("dve"), 1)
    dve.drain().then_inc(K.phase_met, 1)
    dve.wait_ge(K.phase_met, K.phase_end("dve"))
    for t in range(NT):
        dve_rotate(K, dve, V["bqk"][:, t, :].rearrange("p (h c) -> p h c", h=2 * B_H),
                   V["rot"][:, t, :].rearrange("p (h c) -> p h c", h=2 * B_H), 2 * B_H, 32, 0, t, V["rot_tmp"])
        k = V["rot"][:, t, 256:512]
        dve.tensor_scalar(k, k, B_K ** -0.5, None, ALU.mult).then_inc(K.one_more("dve"), 1)
        dve.wait_ge(K.steps["dve"], K.step_n["dve"])
        ins = dve.tensor_tensor(V["kz"][:, t, :].rearrange("p (h c) -> p h c", h=B_H),
                                k.rearrange("p (h c) -> p h c", h=B_H), over(K.const("zeta"), 64, 2), ALU.mult)
        if t < NT - 1:
            ins.then_inc(K.one_more("dve"), 1)
        else:
            ins.then_inc(K.rotated, 1)
    dve.wait_ge(K.free_of((s, "rot", 1)), K.turn((s, "rot", 1)))
    for c in range(2):
        dve.tensor_tensor(V["qx_t"][:, c, :].rearrange("p (t i) -> p t i", t=NT),
                                             V["qk_t"][:, c, :].rearrange("p (t i) -> p t i", t=NT),
                                             over(K.const(f"xi{c}"), NT), ALU.mult).then_inc(K.one_more("dve"), 1)
        dve.wait_ge(K.steps["dve"], K.step_n["dve"])
    for t in range(NT):
        dve.wait_ge(K.full_of((s, "u", t)), K.turn((s, "u", t)))
        bank = K.bank((s, "u", t))
        for c in range(2):
            u = bank[:, c * P:(c + 1) * P]
            nxt = V["state"][:, c * NT + t + 1, :] if t < NT - 1 else V["rot_tmp"][:, 0, 0:P]
            if t == 0:
                ins = dve.tensor_copy(nxt, u)
            else:
                ins = dve.scalar_tensor_tensor(nxt, V["state"][:, c * NT + t, :], K.const("gchunk")[:, c:c + 1], u,
                                               ALU.mult, ALU.add)
            if c == 0:
                ins.then_inc(K.one_more("dve"), 1)
                dve.wait_ge(K.steps["dve"], K.step_n["dve"])
            else:
                ins.then_inc(K.free_of((s, "u", t)), 1)
        dve.wait_ge(K.free_of((s, "u", t)), K.turn((s, "u", t)))
    for t in range(NT):
        for par in range(2):
            dve.wait_ge(K.full_of((s, "qk", t, par)), K.turn((s, "qk", t, par)))
            bank = K.bank((s, "qk", t, par))
            for c in range(2):
                h = 2 * c + par
                ins = dve.tensor_tensor(V["sd_t"][:, t * B_H + h, :], bank[:, c * P:(c + 1) * P],
                                        K.const(f"decay{h}"), ALU.mult)
                if c == 0:
                    ins.then_inc(K.one_more("dve"), 1)
                    dve.wait_ge(K.steps["dve"], K.step_n["dve"])
                else:
                    ins.then_inc(K.free_of((s, "qk", t, par)), 1)
        if t == 0:
            dve.tensor_copy(K.stat[:, 76:77], K.stat[:, 0:1]).then_inc(K.retention_states, 1)
    for t in range(NT):
        for par in range(2):
            dve.wait_ge(K.free_of((s, "r", t, par)), K.turn((s, "r", t, par)))
        for h in range(B_H):
            n = t * B_H + h
            dve.bn_stats(K.stat[:, 112 + 6 * n:118 + 6 * n],
                                            V["mixed"][:, t, 512 + h * P:512 + (h + 1) * P]).then_inc(K.one_more("dve"), 1)
            dve.wait_ge(K.steps["dve"], K.step_n["dve"])
            dve.bn_aggr(K.stat[:, 208 + 2 * n:210 + 2 * n], K.stat[:, 112 + 6 * n:118 + 6 * n]).then_inc(K.one_more("dve"), 1)
    dve.wait_ge(K.steps["dve"], K.step_n["dve"])
    dve.tensor_copy(K.stat[:, 80:96], K.stat[:, 209:240:2]).then_inc(K.group_variances, 1)
    dve.wait_ge(K.group_deviations, 1)
    dve.reciprocal(K.stat[:, 240:256], K.stat[:, 96:112]).then_inc(K.one_more("dve"), 1)
    dve.wait_ge(K.steps["dve"], K.step_n["dve"])
    for t in range(NT):
        for h in range(B_H):
            n = t * B_H + h
            m = V["mixed"][:, t, 512 + h * P:512 + (h + 1) * P]
            dve.tensor_scalar(m, m, K.stat[:, 208 + 2 * n:209 + 2 * n], K.stat[:, 240 + n:241 + n],
                                            ALU.subtract, ALU.mult).then_inc(K.one_more("dve"), 1)
    dve.wait_ge(K.steps["dve"], K.step_n["dve"])
    for t in range(NT):
        m = V["mixed"][:, t, 512:1024]
        dve.tensor_tensor(m, m, V["bg"][:, t, :], ALU.mult).then_inc(K.one_more("dve"), 1)
    dve.drain().then_inc(K.phase_met, 1)
    dve.wait_ge(K.phase_met, K.phase_end("dve"))
    dve_mix_out(K, dve, s, V["proj"])
    dve.drain().then_inc(K.phase_met, 1)
    dve.wait_ge(K.phase_met, K.phase_end("dve"))

def odd_views(K):
    V, e = {}, 0
    for name, shape in (("cq_t", (4, T)), ("ck_t", (4, T)), ("cv", (NT, 512)), ("cg", (NT, 512)), ("o1", (NT, 512)),
                        ("o2", (NT, 512)), ("mixed", (NT, D))):
        V[name], e = K.carve(e, *shape)
    V["att"] = attention_buffers(K, e)[:3]
    e += 6 * T
    V["dg"], e = K.carve(e, NT, 512)
    V["lat"], e = K.carve(e, NT, M_QL + M_KL + M_R)
    V["rot_tmp"], _ = K.carve(e, 4, 256)
    e = 0
    for name, shape in (("lat_t", (3, T)), ("qd", (NT, M_H * M_Q)), ("kv", (NT, M_H * (M_N + M_V))),
                        ("k_full", (NT, M_H * M_Q))):
        V[name], e = K.carve(e, *shape)
    V["k_t"], _ = K.carve(0, M_H, T)
    V["proj"], e = K.carve(0, NT, D)
    V["junk"], e = K.carve(e, NT, D)
    V["normed"], _ = K.carve(0, NT, D)
    return V


def diff_steps(K, V):
    steps = []
    for h in range(C_H):
        for half, out in ((0, "o1"), (1, "o2")):
            p = 64 * half
            for i in range(NT):
                nk = (i + 1) * P
                steps.append(dict(q=V["cq_t"][p:p + 64, h, i * P:nk], k=V["ck_t"][p:p + 64, h, 0:nk],
                                  v=lambda kb, h=h: V["cv"][:, kb, h * P:(h + 1) * P],
                                  bias=K.const("causal")[:, T - nk:T], scale=C_K ** -0.5,
                                  out=V[out][:, i, h * P:(h + 1) * P]))
    return steps


def mla_steps(K, V):
    steps = []
    for h in range(M_H):
        for i in range(NT):
            nk = (i + 1) * P
            v0 = h * (M_N + M_V) + M_N
            steps.append(dict(q=K.h_t[0:M_Q, h, i * P:nk], k=V["k_t"][0:M_Q, h, 0:nk],
                              v=lambda kb, v0=v0: V["kv"][:, kb, v0:v0 + M_V],
                              bias=K.const("causal")[:, T - nk:T], scale=M_Q ** -0.5,
                              out=V["mixed"][:, i, 512 + h * M_V:512 + (h + 1) * M_V]))
    return steps


def pe_odd(K, pe, s):
    V = odd_views(K)
    pe_norm(K, pe, (s, "norm"), V["normed"])
    pe.drain().then_inc(K.phase_met, 1)
    pe.wait_ge(K.phase_met, K.phase_end("pe"))
    for name in ("cq", "ck"):
        blk = K.next_block()
        pe.wait_ge(K.weight_landed[blk % SLOTS], K.landed_at[blk])
        pe_feature_major(K, pe, (s, name), K.h_t, [0, P, 2 * P, 3 * P], blk)
    for name in ("cv", "cg"):
        blk = K.next_block()
        pe.wait_ge(K.weight_landed[blk % SLOTS], K.landed_at[blk])
        pe_token_major(K, pe, (s, name), K.h_t, 512, blk=blk)
    blk = K.next_block()
    pe.wait_ge(K.weight_landed[blk % SLOTS], K.landed_at[blk])
    pe_token_major(K, pe, (s, "lat"), K.h_t, M_QL + M_KL + M_R, blk=blk)
    blk = K.next_block()
    pe.wait_ge(K.weight_landed[blk % SLOTS], K.landed_at[blk])
    pe_token_major(K, pe, (s, "dg"), K.h_t, 512, blk=blk)
    pe.drain().then_inc(K.phase_met, 1)
    pe.wait_ge(K.phase_met, K.phase_end("pe"))
    pe_attention(K, pe, "c", diff_steps(K, V), V["att"])
    pe.drain().then_inc(K.phase_met, 1)
    pe.wait_ge(K.phase_met, K.phase_end("pe"))
    pe.wait_ge(K.latents_normed, 1)
    for c in range(3):
        pe_transpose(K, pe, (s, "lat_t", c), lambda t, c=c: V["lat"][:, t, c * P:(c + 1) * P])
    pe.wait_ge(K.free_of((s, "lat_t", 2)), K.turn((s, "lat_t", 2)))
    blk = K.next_block()
    pe.wait_ge(K.weight_landed[blk % SLOTS], K.landed_at[blk])
    slot = K.ring[:, blk % SLOTS]
    uq = slot[:, 0:3, :].rearrange("p a b -> p (a b)").rearrange("p (k c) -> p k c", k=2)
    ukv = slot[:, 3:5, :].rearrange("p a b -> p (a b)")
    for t in range(NT):
        for n, (c0, c1) in enumerate(((0, 512), (512, 768))):
            bank = K.next_bank((s, "uq", t, n))
            if K.turn((s, "uq", t, n)) > 1:
                pe.wait_ge(K.free_of((s, "uq", t, n)), K.turn((s, "uq", t, n)) - 1)
            for k in range(2):
                last = pe.matmul(bank[:, 0:c1 - c0], V["lat_t"][:, k, t * P:(t + 1) * P], uq[:, k, c0:c1],
                                 start=(k == 0), stop=(k == 1))
                if t == n == k == 0:
                    last.then_inc(K.weights_used, 1)
            last.then_inc(K.full_of((s, "uq", t, n)), 1)
    for t in range(NT):
        for n in range(2):
            bank = K.next_bank((s, "ukv", t, n))
            if K.turn((s, "ukv", t, n)) > 1:
                pe.wait_ge(K.free_of((s, "ukv", t, n)), K.turn((s, "ukv", t, n)) - 1)
            pe.matmul(bank, V["lat_t"][:, 2, t * P:(t + 1) * P], ukv[:, n * 512:(n + 1) * 512],
                               start=True, stop=True).then_inc(K.full_of((s, "ukv", t, n)), 1)
    pe.wait_ge(K.queries_rotated, 1)
    for h in range(M_H):
        pe_transpose(K, pe, (s, "q_t", h), lambda t, h=h: V["qd"][:, t, h * M_Q:(h + 1) * M_Q], M_Q)
    pe.wait_ge(K.keys_whole, 1)
    for h in range(M_H):
        pe_transpose(K, pe, (s, "k_t", h), lambda t, h=h: V["k_full"][:, t, h * M_Q:(h + 1) * M_Q], M_Q)
    pe.drain().then_inc(K.phase_met, 1)
    pe.wait_ge(K.phase_met, K.phase_end("pe"))
    pe_attention(K, pe, "m", mla_steps(K, V), V["att"])
    pe.drain().then_inc(K.phase_met, 1)
    pe.wait_ge(K.phase_met, K.phase_end("pe"))
    pe_mix_out(K, pe, s, V["mixed"])
    pe.drain().then_inc(K.phase_met, 1)
    pe.wait_ge(K.phase_met, K.phase_end("pe"))


def act_odd(K, act, s):
    V = odd_views(K)
    act_norm(K, act, K.x_res, V["junk"])
    act_norm_out(K, act, (s, "norm"), K.gains_at["pre_norm"] + KD)
    act.drain().then_inc(K.phase_met, 1)
    act.wait_ge(K.phase_met, K.phase_end("act"))
    for name, dst in (("cq", "cq_t"), ("ck", "ck_t")):
        for c in range(4):
            act.wait_ge(K.full_of(((s, name), c)), K.turn(((s, name), c)))
            act.copy(V[dst][:, c, :], K.bank(((s, name), c))).then_inc(K.free_of(((s, name), c)), 1)
    for name, func, n in (("cv", ACT.Copy, 512), ("cg", ACT.Silu, 512), ("lat", ACT.Copy, M_QL + M_KL + M_R),
                          ("dg", ACT.Silu, 512)):
        for t in range(NT):
            act.wait_ge(K.full_of(((s, name), t)), K.turn(((s, name), t)))
            act.activation(V[name][:, t, :], K.bank(((s, name), t))[:, 0:n], func).then_inc(K.free_of(((s, name), t)), 1)
    act.drain().then_inc(K.phase_met, 1)
    act.wait_ge(K.phase_met, K.phase_end("act"))
    act_attention(K, act, "c", diff_steps(K, V), V["att"])
    act.drain().then_inc(K.phase_met, 1)
    act.wait_ge(K.phase_met, K.phase_end("act"))
    junk = V["cq_t"]
    for t in range(NT):
        act.activation(junk[:, t, 0:M_QL], V["lat"][:, t, 0:M_QL], ACT.Square,
                                     accum_out=K.stat[:, 40 + t:41 + t]).then_inc(K.one_more("act"), 1)
        act.activation(junk[:, t, M_QL:M_QL + M_KL], V["lat"][:, t, M_QL:M_QL + M_KL], ACT.Square,
                                     accum_out=K.stat[:, 44 + t:45 + t]).then_inc(K.one_more("act"), 1)
    act.wait_ge(K.steps["act"], K.step_n["act"])
    act.activation(K.stat[:, 48:52], K.stat[:, 40:44], ACT.Sqrt, bias=K.eps[:, 0:1], scale=1.0 / M_QL).then_inc(K.one_more("act"), 1)
    act.activation(K.stat[:, 52:56], K.stat[:, 44:48], ACT.Sqrt, bias=K.eps[:, 0:1], scale=1.0 / M_KL).then_inc(K.latent_squares, 1)
    act.wait_ge(K.heads_subtracted, 1)
    for t in range(NT):
        for h in range(C_H):
            n = t * C_H + h
            act.activation(junk[:, t, h * P:(h + 1) * P], V["o1"][:, t, h * P:(h + 1) * P], ACT.Square,
                                         accum_out=K.stat[:, 80 + n:81 + n]).then_inc(K.one_more("act"), 1)
    act.wait_ge(K.steps["act"], K.step_n["act"])
    act.activation(K.stat[:, 96:112], K.stat[:, 80:96], ACT.Sqrt, bias=K.eps[:, 0:1], scale=1.0 / C_V).then_inc(K.head_squares, 1)
    act.wait_ge(K.heads_normed, 1)
    for c in range(3):
        gain = K.gains_at["mla_q_norm"] + c if c < 2 else K.gains_at["mla_kv_norm"]
        act.wait_ge(K.full_of((s, "lat_t", c)), K.turn((s, "lat_t", c)))
        bank = K.bank((s, "lat_t", c))
        act.activation(V["lat_t"][:, c, :], bank, ACT.Copy, scale=K.gains[:, gain:gain + 1]).then_inc(K.free_of((s, "lat_t", c)), 1)
        act.wait_ge(K.free_of((s, "lat_t", c)), K.turn((s, "lat_t", c)))
    for t in range(NT):
        for n, (c0, c1) in enumerate(((0, 512), (512, 768))):
            act.wait_ge(K.full_of((s, "uq", t, n)), K.turn((s, "uq", t, n)))
            act.copy(V["qd"][:, t, c0:c1], K.bank((s, "uq", t, n))[:, 0:c1 - c0]).then_inc(K.free_of((s, "uq", t, n)), 1)
    for t in range(NT):
        for n in range(2):
            act.wait_ge(K.full_of((s, "ukv", t, n)), K.turn((s, "ukv", t, n)))
            act.copy(V["kv"][:, t, n * 512:(n + 1) * 512], K.bank((s, "ukv", t, n))).then_inc(K.free_of((s, "ukv", t, n)), 1)
    for h in range(M_H):
        act.wait_ge(K.full_of((s, "q_t", h)), K.turn((s, "q_t", h)))
        act.copy(K.h_t[0:M_Q, h, :], K.bank((s, "q_t", h))[0:M_Q, :]).then_inc(K.free_of((s, "q_t", h)), 1)
    for h in range(M_H):
        act.wait_ge(K.full_of((s, "k_t", h)), K.turn((s, "k_t", h)))
        act.copy(V["k_t"][0:M_Q, h, :], K.bank((s, "k_t", h))[0:M_Q, :]).then_inc(K.free_of((s, "k_t", h)), 1)
    act.drain().then_inc(K.phase_met, 1)
    act.wait_ge(K.phase_met, K.phase_end("act"))
    act_attention(K, act, "m", mla_steps(K, V), V["att"])
    act.drain().then_inc(K.phase_met, 1)
    act.wait_ge(K.phase_met, K.phase_end("act"))
    act_mix_out(K, act, s, V["proj"], V["junk"])
    act.drain().then_inc(K.phase_met, 1)
    act.wait_ge(K.phase_met, K.phase_end("act"))


def dve_odd(K, dve, s):
    V = odd_views(K)
    dve_norm(K, dve, K.x_res, V["normed"])
    dve.drain().then_inc(K.phase_met, 1)
    dve.wait_ge(K.phase_met, K.phase_end("dve"))
    dve.drain().then_inc(K.phase_met, 1)
    dve.wait_ge(K.phase_met, K.phase_end("dve"))
    dve_attention(K, dve, "c", diff_steps(K, V), V["att"])
    dve.drain().then_inc(K.phase_met, 1)
    dve.wait_ge(K.phase_met, K.phase_end("dve"))
    dve.wait_ge(K.latent_squares, 1)
    dve.reciprocal(K.stat[:, 56:64], K.stat[:, 48:56]).then_inc(K.one_more("dve"), 1)
    dve.wait_ge(K.steps["dve"], K.step_n["dve"])
    for t in range(NT):
        for n, (c0, c1) in enumerate(((0, M_QL), (M_QL, M_QL + M_KL))):
            lat = V["lat"][:, t, c0:c1]
            ins = dve.tensor_scalar(lat, lat, K.stat[:, 56 + 4 * n + t:57 + 4 * n + t], None, ALU.mult)
            if (t, n) != (NT - 1, 1):
                ins.then_inc(K.one_more("dve"), 1)
            else:
                ins.then_inc(K.latents_normed, 1)
    lam = K.lam
    for t in range(NT):
        dve.scalar_tensor_tensor(V["o1"][:, t, :], V["o2"][:, t, :], lam[:, 4:5], V["o1"][:, t, :],
                                               ALU.mult, ALU.add).then_inc(K.one_more("dve"), 1)
    dve.wait_ge(K.steps["dve"], K.step_n["dve"])
    dve.tensor_copy(K.stat[:, 76:77], K.stat[:, 56:57]).then_inc(K.heads_subtracted, 1)
    dve.wait_ge(K.head_squares, 1)
    dve.reciprocal(K.stat[:, 112:128], K.stat[:, 96:112]).then_inc(K.one_more("dve"), 1)
    dve.wait_ge(K.steps["dve"], K.step_n["dve"])
    for t in range(NT):
        for h in range(C_H):
            n = t * C_H + h
            o = V["o1"][:, t, h * P:(h + 1) * P]
            dve.scalar_tensor_tensor(o, o, K.stat[:, 112 + n:113 + n], K.small_rows[:, 0:P],
                                                   ALU.mult, ALU.mult).then_inc(K.one_more("dve"), 1)
    dve.wait_ge(K.steps["dve"], K.step_n["dve"])
    for t in range(NT):
        ins = dve.scalar_tensor_tensor(V["mixed"][:, t, 0:512], V["o1"][:, t, :], 1.0 - LAM_INIT, V["cg"][:, t, :],
                                       ALU.mult, ALU.mult)
        if t < NT - 1:
            ins.then_inc(K.one_more("dve"), 1)
        else:
            ins.then_inc(K.heads_normed, 1)
    for t in range(NT):
        for n in range(2):
            dve.wait_ge(K.free_of((s, "uq", t, n)), K.turn((s, "uq", t, n)))
    for t in range(NT):
        rope = V["qd"][:, t, :].rearrange("p (h c) -> p h c", h=M_H)[:, :, M_N:M_Q]
        dve_rotate(K, dve, rope, rope, M_H, 16, 32, t, V["rot_tmp"])
    dve.tensor_copy(K.stat[:, 77:78], K.stat[:, 56:57]).then_inc(K.queries_rotated, 1)
    for t in range(NT):
        rope = V["lat"][:, t, M_QL + M_KL:M_QL + M_KL + M_R].rearrange("p (h c) -> p h c", h=1)
        dve_rotate(K, dve, rope, rope, 1, 16, 32, t, V["rot_tmp"])
        for n in range(2):
            dve.wait_ge(K.free_of((s, "ukv", t, n)), K.turn((s, "ukv", t, n)))
        full = V["k_full"][:, t, :].rearrange("p (h c) -> p h c", h=M_H)
        dve.tensor_copy(full[:, :, 0:M_N],
                                      V["kv"][:, t, :].rearrange("p (h c) -> p h c", h=M_H)[:, :, 0:M_N]).then_inc(K.one_more("dve"), 1)
        ins = dve.tensor_copy(full[:, :, M_N:M_Q], rope.to_broadcast([P, M_H, M_R]))
        ins.then_inc(K.one_more("dve"), 1)
        dve.wait_ge(K.steps["dve"], K.step_n["dve"])
    dve.tensor_copy(K.stat[:, 78:79], K.stat[:, 56:57]).then_inc(K.keys_whole, 1)
    dve.drain().then_inc(K.phase_met, 1)
    dve.wait_ge(K.phase_met, K.phase_end("dve"))
    dve_attention(K, dve, "m", mla_steps(K, V), V["att"])
    for t in range(NT):
        m = V["mixed"][:, t, 512:1024]
        dve.tensor_tensor(m, m, V["dg"][:, t, :], ALU.mult).then_inc(K.one_more("dve"), 1)
    dve.drain().then_inc(K.phase_met, 1)
    dve.wait_ge(K.phase_met, K.phase_end("dve"))
    dve_mix_out(K, dve, s, V["proj"])
    dve.drain().then_inc(K.phase_met, 1)
    dve.wait_ge(K.phase_met, K.phase_end("dve"))

DK = 128
NC = T // CH


def mix_views(K):
    V = {}
    V["q"], e = K.carve(0, 4, T)
    V["b"], e = K.carve(e, 4, T)
    V["k"], e = K.carve(e, 4, T)
    V["v"], e = K.carve(e, NT, 512)
    V["w"], e = K.carve(e, 2, 4 * T)
    V["s_t"], e = K.carve(e, 16, P)
    assert e == 14336
    V["state"], e = K.carve(e, 32, P)
    V["o"], e = K.carve(e, NT, D)
    V["gate"], e = K.carve(e, NT, 512)
    V["b_end"], e = K.carve(e, 1, 32)
    V["lb"], e = K.carve(e, 6, 8)
    V["o_t"], e = K.carve(0, KD, T)
    V["gate_y"], e = K.carve(e, NT, D)
    V["y"], e = K.carve(e, NT, D)
    V["pad"], e = K.carve(0, 4, T + 3)
    V["acc"], e = K.carve(e, 4, T)
    V["c_v"], e = K.carve(e, 4, T)
    mats_end = e
    V["c_qk"], e = K.carve(e, 4, T)
    V["z"], e = K.carve(e, NT, 512)
    V["k_tok"], e = K.carve(e, NT, 256)
    V["v_tok"], e = K.carve(e, NT, 512)
    V["o_tok"], e = K.carve(e, NT, 512)
    more = e
    names = ["gb", "eg0", "lt", "qk0", "at", "al0", "al1", "tt", "rr0", "xx", "rn", "wn0", "qe0", "kte0", "vn", "s",
             "eg1", "qk1", "rr1", "wn1", "qe1", "kte1"]
    at = 0
    for name in names:
        if at + 512 > mats_end and at < more:
            at = more
        V["m_" + name], at = K.carve(at, 4, P)
    V["gd"], at = K.carve(at, 6, 64)
    V["sc"], at = K.carve(at, 1, 8)
    V["sc16"] = K.sc16[:]
    V["gd_raw"] = K.gd_raw[:]
    V["og_t"], end = K.carve(K.ARENA - 2 * KD * T, 2 * KD, T)
    assert at <= K.ARENA - 2 * KD * T, at
    V["gate_g"], e = K.carve(0, NT, D)
    V["y2"], e = K.carve(e, NT, D)
    V["y_h"], e = K.carve(e, NT, D)
    V["normed"], e = K.carve(0, NT, D)
    V["junk"], _ = K.carve(e, NT, D)
    return V


def halves(ap, m):
    return ap.rearrange("p (n r m) -> p n r m", r=2, m=m)


def pe_mix(K, pe, s):
    V = mix_views(K)
    pe_norm(K, pe, (s, "norm"), V["normed"])
    pe.drain().then_inc(K.phase_met, 1)
    pe.wait_ge(K.phase_met, K.phase_end("pe"))
    blk = K.next_block()
    pe.wait_ge(K.weight_landed[blk % SLOTS], K.landed_at[blk])
    pe_feature_major(K, pe, (s, "hf", 0), K.h_t, [0, P, 2 * P, 3 * P], blk)
    for g in range(2):
        blk = K.next_block()
        pe.wait_ge(K.weight_landed[blk % SLOTS], K.landed_at[blk])
        pe_feature_major(K, pe, (s, "hq", g), K.h_t, [0, P, 2 * P, 3 * P], blk)
        blk = K.next_block()
        pe.wait_ge(K.weight_landed[blk % SLOTS], K.landed_at[blk])
        pe_token_major(K, pe, (s, "hi", g), K.h_t, 512, blk=blk, tiles=[0, 1])
        for lv in range(LEVELS + 1):
            if lv < LEVELS:
                pe.wait_ge(K.hgrn_factors, g * LEVELS + lv + 1)
                w = V["w"][:, lv % 2, :]
                left, right = w, w
            else:
                left = V["k"].rearrange("p h t -> p (h t)")
                right = V["q"].rearrange("p h t -> p (h t)")
            for h in range(4):
                bank = K.next_bank((s, "hs", g, lv, h))
                if K.turn((s, "hs", g, lv, h)) > 1:
                    pe.wait_ge(K.free_of((s, "hs", g, lv, h)), K.turn((s, "hs", g, lv, h)) - 1)
                for j in range(NT):
                    c = slice(h * T + j * P, h * T + (j + 1) * P)
                    last = pe.matmul(bank[:, j * P:(j + 1) * P], left[:, c], right[:, c], start=True, stop=True)
                last.then_inc(K.full_of((s, "hs", g, lv, h)), 1)
            if lv < 2:
                pe_token_major(K, pe, (s, "hi", g), K.h_t, 512, blk=blk, tiles=[2 + lv])
            elif lv < LEVELS:
                if lv == 2:
                    blk = K.next_block()
                    pe.wait_ge(K.weight_landed[blk % SLOTS], K.landed_at[blk])
                pe_token_major(K, pe, (s, "hg", g), K.h_t, 512, blk=blk, tiles=[lv - 2])
        pe.drain().then_inc(K.phase_met, 1)
        pe.wait_ge(K.phase_met, K.phase_end("pe"))
        pe.wait_ge(K.hgrn_k_to_end, g + 1)
        for h in range(4):
            bank = K.next_bank((s, "ke", g, h))
            if K.turn((s, "ke", g, h)) > 1:
                pe.wait_ge(K.free_of((s, "ke", g, h)), K.turn((s, "ke", g, h)) - 1)
            for j in range(NT):
                last = pe.transpose(bank[:, j * P:(j + 1) * P], V["w"][:, 1, h * T + j * P:h * T + (j + 1) * P],
                                    K.const("ident"))
            last.then_inc(K.full_of((s, "ke", g, h)), 1)
        for h in range(4):
            pe.wait_ge(K.free_of((s, "ke", g, h)), K.turn((s, "ke", g, h)))
            for par in range(2):
                p = CH * par
                bank = K.next_bank((s, "hu", g, h, par))
                if K.turn((s, "hu", g, h, par)) > 1:
                    pe.wait_ge(K.free_of((s, "hu", g, h, par)), K.turn((s, "hu", g, h, par)) - 1)
                for j in range(NT):
                    last = pe.matmul(bank[:, j * P:(j + 1) * P], V["k"][p:p + CH, h, j * P:(j + 1) * P],
                                     V["v"][p:p + CH, j, h * P:(h + 1) * P], start=True, stop=True)
                last.then_inc(K.full_of((s, "hu", g, h, par)), 1)
        pe.wait_ge(K.hgrn_states, g + 1)
        for j in range(NT):
            bank = K.next_bank((s, "ho", g, j))
            if K.turn((s, "ho", g, j)) > 1:
                pe.wait_ge(K.free_of((s, "ho", g, j)), K.turn((s, "ho", g, j)) - 1)
            for h in range(4):
                o = bank[:, h * P:(h + 1) * P]
                last = pe.matmul(o, V["s_t"][:, h * NT + j, :], V["v"][:, j, h * P:(h + 1) * P], start=True,
                                 stop=False)
                for c in (2 * j, 2 * j + 1):
                    p = CH * (c % 2)
                    last = pe.matmul(o[p:p + CH, :], V["w"][:, 0, h * T + c * CH:h * T + (c + 1) * CH],
                                     V["state"][:, h * NC + c, :], start=False, stop=True)
            last.then_inc(K.full_of((s, "ho", g, j)), 1)
        pe.drain().then_inc(K.phase_met, 1)
        blk = K.next_block()
        pe.wait_ge(K.weight_landed[blk % SLOTS], K.landed_at[blk])
        if g == 0:
            pe_feature_major(K, pe, (s, "hf", 1), K.h_t, [0, P, 2 * P, 3 * P], blk)
        else:
            pe_token_major(K, pe, (s, "gate_h", 0), K.h_t, 512, blk=blk)
        pe.wait_ge(K.phase_met, K.phase_end("pe"))
    pe.wait_ge(K.hgrn_gated, 2)
    for kt in range(KD):
        pe_transpose(K, pe, (s, "o_t", kt), lambda t, kt=kt: V["o"][:, t, kt * P:(kt + 1) * P])
    blk = K.next_block()
    pe.wait_ge(K.weight_landed[blk % SLOTS], K.landed_at[blk])
    pe_token_major(K, pe, (s, "gate_h", 1), K.h_t, 512, blk=blk)
    pe.wait_ge(K.free_of((s, "o_t", KD - 1)), K.turn((s, "o_t", KD - 1)))
    pe_square(K, pe, (s, "y_h"), V["o_t"])
    blk = K.next_block()
    pe.wait_ge(K.weight_landed[blk % SLOTS], K.landed_at[blk])
    pe_token_major(K, pe, (s, "gab"), K.h_t, 32, blk=blk)
    pe.drain().then_inc(K.phase_met, 1)
    blk = K.next_block()
    pe.wait_ge(K.weight_landed[blk % SLOTS], K.landed_at[blk])
    pe_feature_major(K, pe, (s, "gqk", 0), K.h_t, [0, P, 2 * P, 3 * P], blk)
    pe.wait_ge(K.phase_met, K.phase_end("pe"))
    pe.wait_ge(K.gdn_decays, 1)
    bank = K.next_bank((s, "gam"))
    if K.turn((s, "gam")) > 1:
        pe.wait_ge(K.free_of((s, "gam")), K.turn((s, "gam")) - 1)
    for j in range(NT):
        last = pe.matmul(bank[:, j * 16:(j + 1) * 16], K.const("cum"), V["gd"][:, 0, j * 16:(j + 1) * 16],
                         start=True, stop=True)
    last.then_inc(K.full_of((s, "gam")), 1)
    for g in range(4):
        blk = K.next_block()
        pe.wait_ge(K.weight_landed[blk % SLOTS], K.landed_at[blk])
        pe_feature_major(K, pe, (s, "gv", g), K.h_t, [0, P, 2 * P, 3 * P], blk)
        pe.drain().then_inc(K.phase_met, 1)
        blk = K.next_block()
        pe.wait_ge(K.weight_landed[blk % SLOTS], K.landed_at[blk])
        pe_token_major(K, pe, (s, "gz", g), K.h_t, 512, blk=blk, tiles=[0, 1])
        pe.wait_ge(K.phase_met, K.phase_end("pe"))
        for m in range(2):
            bank = K.next_bank((s, "qk_sum", g, m))
            if K.turn((s, "qk_sum", g, m)) > 1:
                pe.wait_ge(K.free_of((s, "qk_sum", g, m)), K.turn((s, "qk_sum", g, m)) - 1)
            for r in range(2):
                n = 2 * m + r
                pe.wait_ge(K.qk_squares, 4 * g + n + 1)
                last = pe.matmul(bank[64 * r:64 * (r + 1), :], K.const("ones")[:, 0:64], V["acc"][:, n, :],
                                 start=True, stop=True)
            last.then_inc(K.full_of((s, "qk_sum", g, m)), 1)
        pe_token_major(K, pe, (s, "gz", g), K.h_t, 512, blk=blk, tiles=[2])
        for n in range(4):
            bank = K.next_bank((s, "qk_scale", g, n))
            if K.turn((s, "qk_scale", g, n)) > 1:
                pe.wait_ge(K.free_of((s, "qk_scale", g, n)), K.turn((s, "qk_scale", g, n)) - 1)
            pe.wait_ge(K.qk_inverted, 2 * g + n // 2 + 1)
            col = 64 * (n % 2)
            pe.matmul(bank, K.const("ident")[:, col:col + 1].to_broadcast([P, P]), V["pad"][:, n // 2, 0:T],
                      start=True, stop=True).then_inc(K.full_of((s, "qk_scale", g, n)), 1)
        for n in range(4):
            pe_transpose(K, pe, (s, "v_tok", g, n), lambda t, n=n: V["c_v"][:, n, t * P:(t + 1) * P])
        for n in range(2):
            pe.wait_ge(K.free_of((s, "qk_scale", g, 2 + n)), K.turn((s, "qk_scale", g, 2 + n)))
            pe_transpose(K, pe, (s, "k_tok", g, n), lambda t, n=n: V["c_qk"][:, 2 + n, t * P:(t + 1) * P])
        pe.drain().then_inc(K.phase_met, 1)
        pe.wait_ge(K.phase_met, K.phase_end("pe"))
        for j, piece, arg in delta_order():
            if piece == "gate":
                pe_token_major(K, pe, (s, "gz", g), K.h_t, 512, blk=blk, tiles=[3])
            pe_delta_piece(K, pe, s, V, g, j, piece, arg)
        pe.drain().then_inc(K.phase_met, 1)
        blk = K.next_block()
        pe.wait_ge(K.weight_landed[blk % SLOTS], K.landed_at[blk])
        if g < 3:
            pe_feature_major(K, pe, (s, "gqk", g + 1), K.h_t, [0, P, 2 * P, 3 * P], blk)
        else:
            pe_token_major(K, pe, (s, "gate_g", 0), K.h_t, 512, blk=blk)
        pe.wait_ge(K.phase_met, K.phase_end("pe"))
        pe.wait_ge(K.gdn_gated, g + 1)
        for n in range(4):
            pe_transpose(K, pe, (s, "og_t", g, n), lambda t, n=n: V["o_tok"][:, t, n * P:(n + 1) * P])
    pe.drain().then_inc(K.phase_met, 1)
    pe.wait_ge(K.phase_met, K.phase_end("pe"))
    blk = K.next_block()
    pe.wait_ge(K.weight_landed[blk % SLOTS], K.landed_at[blk])
    pe_token_major(K, pe, (s, "gate_g", 1), K.h_t, 512, blk=blk)
    pe_square(K, pe, (s, "y_g"), V["og_t"], 2 * KD)
    pe.wait_ge(K.branches_added, 1)
    for kt in range(KD):
        pe_transpose(K, pe, (s, "y_t", kt), lambda t, kt=kt: V["y2"][:, t, kt * P:(kt + 1) * P])
    pe.wait_ge(K.free_of((s, "y_t", KD - 1)), K.turn((s, "y_t", KD - 1)))
    pe_square(K, pe, (s, "out"), K.h_t)
    pe.drain().then_inc(K.phase_met, 1)
    pe.wait_ge(K.phase_met, K.phase_end("pe"))


DELTA_ORDER = [("new", "prepare"), ("old", "values", 0), ("new", "inverse"), ("old", "state", 0),
               ("new", "level", 1), ("old", "values", 1), ("new", "doubled", 1), ("new", "level", 2),
               ("old", "state", 1), ("new", "doubled", 2), ("new", "level", 3), ("next", "decays"),
               ("new", "doubled", 3), ("new", "level", 4), ("new", "doubled", 4), ("new", "level", 5),
               ("next", "products"), ("new", "doubled", 5), ("new", "keys")]


def delta_order():
    yield 0, "decays", None
    yield 0, "products", None
    yield 0, "gate", None
    for j in range(-1, NT):
        for side, piece, *arg in DELTA_ORDER:
            tile = j + ("old", "new", "next").index(side)
            if 0 <= tile < NT:
                yield tile, piece, arg[0] if arg else None


def pe_delta_piece(K, pe, s, V, g, j, piece, arg):
    ts = slice(j * P, (j + 1) * P)
    n = g * NT + j
    if piece == "decays":
        bank = K.next_bank((s, "gb", n))
        if K.turn((s, "gb", n)) > 1:
            pe.wait_ge(K.free_of((s, "gb", n)), K.turn((s, "gb", n)) - 1)
        for v in range(4):
            col = j * 16 + 4 * g + v
            last = pe.matmul(bank[:, v * P:(v + 1) * P], V["gd"][:, 0, col:col + 1].to_broadcast([P, P]),
                             K.const("cum"), start=True, stop=True)
        last.then_inc(K.full_of((s, "gb", n)), 1)
    if piece == "products":
        bank = K.next_bank((s, "kq", n))
        if K.turn((s, "kq", n)) > 1:
            pe.wait_ge(K.free_of((s, "kq", n)), K.turn((s, "kq", n)) - 1)
        for m in range(2):
            k = V["c_qk"][:, 2 + m, ts]
            pe.matmul(bank[:, m * P:(m + 1) * P], k, k, start=True, stop=True)
            last = pe.matmul(bank[:, (2 + m) * P:(3 + m) * P], k, V["c_qk"][:, m, ts], start=True, stop=True)
        last.then_inc(K.full_of((s, "kq", n)), 1)
    if piece == "inverse":
        pe.wait_ge(K.rr_ready, n + 1)
        bank = K.next_bank((s, "t0", n))
        if K.turn((s, "t0", n)) > 1:
            pe.wait_ge(K.free_of((s, "t0", n)), K.turn((s, "t0", n)) - 1)
        for v in range(4):
            last = pe.transpose(bank[:, v * P:(v + 1) * P], V[f"m_rr{n % 2}"][:, v, :], K.const("ident"))
        last.then_inc(K.full_of((s, "t0", n)), 1)
    if piece == "level":
        lv = arg
        pe.wait_ge(K.level_ready, n * (LEVELS - 1) + lv)
        pe.wait_ge(K.free_of((s, "t0", n) if lv == 1 else (s, "ty", n, lv - 1)), K.turn((s, "t0", n) if lv == 1 else (s, "ty", n, lv - 1)))
        bank = K.next_bank((s, "tx", n, lv))
        if K.turn((s, "tx", n, lv)) > 1:
            pe.wait_ge(K.free_of((s, "tx", n, lv)), K.turn((s, "tx", n, lv)) - 1)
        for v in range(4):
            last = pe.matmul(bank[:, v * P:(v + 1) * P], V[f"m_al{lv % 2}"][:, v, :], V["m_tt"][:, v, :],
                             start=True, stop=True)
        last.then_inc(K.full_of((s, "tx", n, lv)), 1)
    if piece == "doubled":
        lv = arg
        pe.wait_ge(K.free_of((s, "tx", n, lv)), K.turn((s, "tx", n, lv)))
        if lv > 1:
            pe.wait_ge(K.free_of((s, "ry", n, lv - 1)), K.turn((s, "ry", n, lv - 1)))
        if lv < LEVELS - 1:
            bank = K.next_bank((s, "ty", n, lv))
            if K.turn((s, "ty", n, lv)) > 1:
                pe.wait_ge(K.free_of((s, "ty", n, lv)), K.turn((s, "ty", n, lv)) - 1)
            for v in range(4):
                last = pe.matmul(bank[:, v * P:(v + 1) * P], V[f"m_rr{n % 2}"][:, v, :], V["m_xx"][:, v, :],
                                 start=True, stop=True)
            last.then_inc(K.full_of((s, "ty", n, lv)), 1)
        bank = K.next_bank((s, "ry", n, lv))
        if K.turn((s, "ry", n, lv)) > 1:
            pe.wait_ge(K.free_of((s, "ry", n, lv)), K.turn((s, "ry", n, lv)) - 1)
        for v in range(4):
            last = pe.matmul(bank[:, v * P:(v + 1) * P], V["m_xx"][:, v, :], V[f"m_rr{n % 2}"][:, v, :],
                             start=True, stop=True)
        last.then_inc(K.full_of((s, "ry", n, lv)), 1)
    if piece == "keys":
        pe.wait_ge(K.rn_ready, n + 1)
        bank = K.next_bank((s, "wn", n))
        if K.turn((s, "wn", n)) > 1:
            pe.wait_ge(K.free_of((s, "wn", n)), K.turn((s, "wn", n)) - 1)
        for v in range(4):
            last = pe.matmul(bank[:, v * P:(v + 1) * P], V["k_tok"][:, j, (v // 2) * P:(v // 2 + 1) * P],
                             V["m_rn"][:, v, :], start=True, stop=True)
        last.then_inc(K.full_of((s, "wn", n)), 1)
    if piece in ("values", "state"):
        c = arg
        p = CH * c
        ps = slice(p, p + CH)
    if piece == "values":
        if c == 0:
            pe.wait_ge(K.free_of((s, "wn", n)), K.turn((s, "wn", n)))
            pe.wait_ge(K.qe_ready, n + 1)
            pe.wait_ge(K.kte_ready, 4 * (n + 1))
        if c:
            pe.wait_ge(K.free_of((s, "su", n, 0)), K.turn((s, "su", n, 0)))
        elif j:
            pe.wait_ge(K.free_of((s, "su", n - 1, 1)), K.turn((s, "su", n - 1, 1)))
        bank = K.next_bank((s, "vn", n, c))
        if K.turn((s, "vn", n, c)) > 1:
            pe.wait_ge(K.free_of((s, "vn", n, c)), K.turn((s, "vn", n, c)) - 1)
        for v in range(4):
            o = bank[ps, v * P:(v + 1) * P]
            pe.matmul(o, V[f"m_rr{n % 2}"][:, v, ps], V["v_tok"][:, j, v * P:(v + 1) * P], start=True, stop=False)
            last = pe.matmul(o, V[f"m_wn{n % 2}"][:, v, ps], V["m_s"][:, v, :], start=False, stop=True)
        last.then_inc(K.full_of((s, "vn", n, c)), 1)
    if piece == "state":
        pe.wait_ge(K.free_of((s, "vn", n, c)), K.turn((s, "vn", n, c)))
        bank = K.next_bank((s, "do", n, c))
        if K.turn((s, "do", n, c)) > 1:
            pe.wait_ge(K.free_of((s, "do", n, c)), K.turn((s, "do", n, c)) - 1)
        for v in range(4):
            o = bank[ps, v * P:(v + 1) * P]
            pe.matmul(o, V[f"m_qe{n % 2}"][:, v, ps], V["m_s"][:, v, :], start=True, stop=False)
            last = pe.matmul(o, V[f"m_qk{n % 2}"][ps, v, ps], V["m_vn"][ps, v, :], start=False, stop=True)
        last.then_inc(K.full_of((s, "do", n, c)), 1)
        bank = K.next_bank((s, "su", n, c))
        if K.turn((s, "su", n, c)) > 1:
            pe.wait_ge(K.free_of((s, "su", n, c)), K.turn((s, "su", n, c)) - 1)
        for v in range(4):
            last = pe.matmul(bank[:, v * P:(v + 1) * P], V[f"m_kte{n % 2}"][ps, v, :], V["m_vn"][ps, v, :],
                             start=True, stop=True)
        last.then_inc(K.full_of((s, "su", n, c)), 1)


HGRN_TILES_AFTER = [[0], [1, 2], [3], [4], [5], [6], [7], []]


def act_mix(K, act, s):
    V = mix_views(K)
    act_norm(K, act, K.x_res, V["junk"])
    act_norm_out(K, act, (s, "norm"), K.gains_at["mix_norm_2"])
    act.drain().then_inc(K.phase_met, 1)
    act.wait_ge(K.phase_met, K.phase_end("act"))
    act.wait_ge(K.lb_shifted, 1)
    act.activation(V["lb"][:, 2:4, :], V["lb"][:, 0:2, :], ACT.Exp).then_inc(K.lb_exps, 1)
    for g in range(2):
        for h in range(4):
            act.wait_ge(K.full_of(((s, "hf", g), h)), K.turn(((s, "hf", g), h)))
            bank = K.bank(((s, "hf", g), h))
            act.activation(V["w"][:, 0, h * T:(h + 1) * T], bank, ACT.Sigmoid).then_inc(K.one_more("act"), 1)
            act.activation(V["k"][:, h, :], bank, ACT.Sigmoid, scale=-1.0).then_inc(K.free_of(((s, "hf", g), h)), 1)
        act.wait_ge(K.hgrn_f, g + 1)
        act.activation(V["w"][:, 0, :], V["w"][:, 0, :], ACT.Ln).then_inc(K.hgrn_log_f, 1)
        for h in range(4):
            act.wait_ge(K.full_of(((s, "hq", g), h)), K.turn(((s, "hq", g), h)))
            act.activation(V["q"][:, h, :], K.bank(((s, "hq", g), h)), ACT.Silu).then_inc(K.free_of(((s, "hq", g), h)), 1)
        for lv in range(LEVELS + 2):
            if lv < LEVELS:
                act.wait_ge(K.hgrn_diffs, g * LEVELS + lv + 1)
                w = V["w"][:, lv % 2, :]
                act.activation(w, w, ACT.Exp).then_inc(K.hgrn_decays, 1)
            for t in HGRN_TILES_AFTER[lv]:
                if t < NT:
                    act.wait_ge(K.full_of(((s, "hi", g), t)), K.turn(((s, "hi", g), t)))
                    act.copy(V["v"][:, t, :], K.bank(((s, "hi", g), t))).then_inc(K.free_of(((s, "hi", g), t)), 1)
                else:
                    t = t - NT
                    act.wait_ge(K.full_of(((s, "hg", g), t)), K.turn(((s, "hg", g), t)))
                    act.activation(V["gate"][:, t, :], K.bank(((s, "hg", g), t)), ACT.Silu).then_inc(K.free_of(((s, "hg", g), t)), 1)
        act.drain().then_inc(K.phase_met, 1)
        act.wait_ge(K.phase_met, K.phase_end("act"))
        act.wait_ge(K.hgrn_to_end, g + 1)
        act.activation(V["w"][:, 0, :], V["b"].rearrange("p h t -> p (h t)"), ACT.Exp).then_inc(K.one_more("act"), 1)
        act.activation(V["b_end"][:, 0, :], V["b"].rearrange("p h (c i) -> p (h c) i", i=CH)[:, :, CH - 1],
                                     ACT.Exp).then_inc(K.one_more("act"), 1)
        act.wait_ge(K.steps["act"], K.step_n["act"])
        act.activation(V["w"][:, 1, :], V["w"][:, 1, :], ACT.Exp).then_inc(K.hgrn_end_decays, 1)
        for h in range(4):
            act.wait_ge(K.full_of((s, "ke", g, h)), K.turn((s, "ke", g, h)))
            act.copy(V["k"][:, h, :], K.bank((s, "ke", g, h))).then_inc(K.free_of((s, "ke", g, h)), 1)
        for j in range(NT):
            dst = V["o"][:, j, g * 512:(g + 1) * 512]
            act.wait_ge(K.full_of((s, "ho", g, j)), K.turn((s, "ho", g, j)))
            act.activation(dst, K.bank((s, "ho", g, j)), ACT.Copy, scale=DK ** -0.5).then_inc(K.free_of((s, "ho", g, j)), 1)
            act.wait_ge(K.free_of((s, "ho", g, j)), K.turn((s, "ho", g, j)))
        act_head_squares(K, act, V["o"], g * 512, V["w"][:, 0, :], K.hgrn_squares)
        act.drain().then_inc(K.phase_met, 1)
        act.wait_ge(K.phase_met, K.phase_end("act"))
    act_gate(K, act, V["gate_y"], (s, "gate_h", 0), 0)
    for kt in range(KD):
        act.wait_ge(K.full_of((s, "o_t", kt)), K.turn((s, "o_t", kt)))
        act.copy(V["o_t"][:, kt, :], K.bank((s, "o_t", kt))).then_inc(K.free_of((s, "o_t", kt)), 1)
        act.wait_ge(K.free_of((s, "o_t", kt)), K.turn((s, "o_t", kt)))
    act_gate(K, act, V["gate_y"], (s, "gate_h", 1), 1)
    for t in range(NT):
        raw = V["gd_raw"][:, t, :]
        act.wait_ge(K.full_of(((s, "gab"), t)), K.turn(((s, "gab"), t)))
        act.copy(raw, K.bank(((s, "gab"), t))[:, 0:32]).then_inc(K.free_of(((s, "gab"), t)), 1)
    act.drain().then_inc(K.phase_met, 1)
    act.wait_ge(K.phase_met, K.phase_end("act"))
    raw, gd = V["gd_raw"], V["gd"]
    act.wait_ge(K.softplus_in, 1)
    act.activation(gd[:, 2, :].rearrange("p (t v) -> p t v", t=NT), raw[:, :, 16:32], ACT.Sigmoid).then_inc(K.one_more("act"), 1)
    act.activation(gd[:, 3, :], gd[:, 1, :], ACT.Abs).then_inc(K.one_more("act"), 1)
    act.wait_ge(K.steps["act"], K.step_n["act"])
    act.activation(gd[:, 3, :], gd[:, 3, :], ACT.Exp, scale=-1.0).then_inc(K.one_more("act"), 1)
    act.activation(V["sc16"], K.small_rows[:, 384:400], ACT.Exp).then_inc(K.softplus_exp, 1)
    act.wait_ge(K.softplus_one, 1)
    act.activation(gd[:, 3, :], gd[:, 3, :], ACT.Ln).then_inc(K.softplus_ln, 1)
    act.wait_ge(K.full_of((s, "gam")), K.turn((s, "gam")))
    bank = K.bank((s, "gam"))
    act.copy(gd[:, 4, :], bank[:, 0:64]).then_inc(K.one_more("act"), 1)
    act.activation(gd[:, 5, :], bank[:, 0:64], ACT.Exp).then_inc(K.free_of((s, "gam")), 1)
    for g in range(4):
        for n in range(8):
            key = ((s, "gqk", g), n) if n < 4 else ((s, "gv", g), n - 4)
            act.wait_ge(K.full_of(key), K.turn(key))
            bank = K.bank(key)
            if n >= 4:
                act.wait_ge(K.conv_done, 8 * g + n - 3)
            act.copy(V["pad"][:, n % 4, 3:T + 3], bank).then_inc(K.free_of(key), 1)
            if n >= 1:
                act_conv_silu(K, act, V, g, n - 1)
        act_conv_silu(K, act, V, g, 7)
        act.drain().then_inc(K.phase_met, 1)
        act.wait_ge(K.phase_met, K.phase_end("act"))
        for n in range(4):
            act.activation(V["acc"][:, n, :], V["c_qk"][:, n, :], ACT.Square).then_inc(K.qk_squares, 1)
        for t in range(2):
            act_silu_gate(K, act, s, V, g, t)
        for m in range(2):
            act.wait_ge(K.full_of((s, "qk_sum", g, m)), K.turn((s, "qk_sum", g, m)))
            act.activation(V["pad"][:, m, 0:T], K.bank((s, "qk_sum", g, m)), ACT.Sqrt,
                           bias=K.eps[:, 0:1]).then_inc(K.free_of((s, "qk_sum", g, m)), 1)
        act_silu_gate(K, act, s, V, g, 2)
        for n in range(4):
            act.wait_ge(K.full_of((s, "v_tok", g, n)), K.turn((s, "v_tok", g, n)))
            src = K.bank((s, "v_tok", g, n)).rearrange("p (t c) -> p t c", t=NT)
            act.copy(V["v_tok"][:, :, n * P:(n + 1) * P], src).then_inc(K.free_of((s, "v_tok", g, n)), 1)
        for n in range(2):
            act.wait_ge(K.full_of((s, "k_tok", g, n)), K.turn((s, "k_tok", g, n)))
            src = K.bank((s, "k_tok", g, n)).rearrange("p (t c) -> p t c", t=NT)
            act.copy(V["k_tok"][:, :, n * P:(n + 1) * P], src).then_inc(K.free_of((s, "k_tok", g, n)), 1)
        act.drain().then_inc(K.phase_met, 1)
        act.wait_ge(K.phase_met, K.phase_end("act"))
        for j, piece, arg in delta_order():
            act_delta_piece(K, act, s, V, g, j, piece, arg)
        for j in range(NT):
            act.wait_ge(K.free_of((s, "do", g * NT + j, 1)), K.turn((s, "do", g * NT + j, 1)))
        act.drain().then_inc(K.phase_met, 1)
        act.wait_ge(K.phase_met, K.phase_end("act"))
        act_head_squares(K, act, V["o_tok"], 0, V["acc"].rearrange("p a b -> p (a b)"), K.gdn_squares)
        for n in range(4):
            act.wait_ge(K.full_of((s, "og_t", g, n)), K.turn((s, "og_t", g, n)))
            act.copy(V["og_t"][:, 4 * g + n, :], K.bank((s, "og_t", g, n))).then_inc(K.free_of((s, "og_t", g, n)), 1)
    act.drain().then_inc(K.phase_met, 1)
    act.wait_ge(K.phase_met, K.phase_end("act"))
    for half in range(2):
        for t in range(NT):
            act.wait_ge(K.full_of(((s, "gate_g", half), t)), K.turn(((s, "gate_g", half), t)))
            act.activation(V["gate_g"][:, t, half * 512:(half + 1) * 512],
                                  K.bank(((s, "gate_g", half), t)), ACT.Sigmoid).then_inc(K.free_of(((s, "gate_g", half), t)), 1)
    for kt in range(KD):
        if kt:
            act.wait_ge(K.free_of((s, "y_t", kt - 1)), K.turn((s, "y_t", kt - 1)))
        act.wait_ge(K.full_of((s, "y_t", kt)), K.turn((s, "y_t", kt)))
        act.copy(K.h_t[:, kt, :], K.bank((s, "y_t", kt))).then_inc(K.free_of((s, "y_t", kt)), 1)
    act.drain().then_inc(K.phase_met, 1)
    act.wait_ge(K.phase_met, K.phase_end("act"))


def act_conv_silu(K, act, V, g, n):
    act.wait_ge(K.conv_done, 8 * g + n + 1)
    dst = V["c_qk"][:, n, :] if n < 4 else V["c_v"][:, n - 4, :]
    act.activation(dst, V["acc"][:, n % 4, :], ACT.Silu).then_inc(K.conv_silu, 1)


def act_silu_gate(K, act, s, V, g, t):
    act.wait_ge(K.full_of(((s, "gz", g), t)), K.turn(((s, "gz", g), t)))
    act.activation(V["z"][:, t, :], K.bank(((s, "gz", g), t)), ACT.Silu).then_inc(K.free_of(((s, "gz", g), t)), 1)


def act_gate(K, act, dst, key, half):
    for t in range(NT):
        act.wait_ge(K.full_of((key, t)), K.turn((key, t)))
        act.activation(dst[:, t, half * 512:(half + 1) * 512], K.bank((key, t)), ACT.Sigmoid).then_inc(K.free_of((key, t)), 1)


def act_head_squares(K, act, src, col, junk, name):
    for t in range(NT):
        for h in range(4):
            n = t * 4 + h
            act.activation(junk[:, n * P:(n + 1) * P], src[:, t, col + h * P:col + (h + 1) * P], ACT.Square,
                                         accum_out=K.stat[:, 80 + n:81 + n]).then_inc(K.one_more("act"), 1)
    act.wait_ge(K.steps["act"], K.step_n["act"])
    act.activation(K.stat[:, 96:112], K.stat[:, 80:96], ACT.Sqrt, bias=K.eps[:, 0:1], scale=1.0 / P).then_inc(name, 1)


def act_delta_piece(K, act, s, V, g, j, piece, arg):
    n = g * NT + j
    flat = lambda name: V[name].rearrange("p v t -> p (v t)")
    if piece == "decays":
        act.wait_ge(K.full_of((s, "gb", n)), K.turn((s, "gb", n)))
        bank = K.bank((s, "gb", n))
        if j >= 2:
            act.wait_ge(K.free_of((s, "su", n - 2, 1)), K.turn((s, "su", n - 2, 1)))
        act.activation(flat(f"m_eg{n % 2}"), bank, ACT.Exp).then_inc(K.one_more("act"), 1)
        act.copy(flat("m_gb"), bank).then_inc(K.free_of((s, "gb", n)), 1)
        act.wait_ge(K.gdn_diff, n + 1)
        act.activation(V["m_lt"], V["m_lt"], ACT.Exp).then_inc(K.gdn_decay, 1)
    if piece == "gate":
        act_silu_gate(K, act, s, V, g, 3)
    if piece == "prepare":
        act.wait_ge(K.end_scales, n + 1)
        for v in range(4):
            act.activation(V[f"m_kte{n % 2}"][:, v, :], V["k_tok"][:, j, (v // 2) * P:(v // 2 + 1) * P], ACT.Copy,
                           scale=V["sc"][:, 0, v:v + 1]).then_inc(K.kte_ready, 1)
    if piece == "inverse":
        act.wait_ge(K.full_of((s, "t0", n)), K.turn((s, "t0", n)))
        act.copy(flat("m_tt"), K.bank((s, "t0", n))).then_inc(K.free_of((s, "t0", n)), 1)
    if piece == "level":
        act.wait_ge(K.full_of((s, "tx", n, arg)), K.turn((s, "tx", n, arg)))
        act.copy(flat("m_xx"), K.bank((s, "tx", n, arg))).then_inc(K.free_of((s, "tx", n, arg)), 1)
    if piece == "keys":
        act.wait_ge(K.full_of((s, "wn", n)), K.turn((s, "wn", n)))
        act.copy(flat(f"m_wn{n % 2}"), K.bank((s, "wn", n))).then_inc(K.free_of((s, "wn", n)), 1)
    if piece == "state":
        p = CH * arg
        act.wait_ge(K.full_of((s, "do", n, arg)), K.turn((s, "do", n, arg)))
        act.copy(V["o_tok"][p:p + CH, j, :],
                 K.bank((s, "do", n, arg))[p:p + CH, :]).then_inc(K.free_of((s, "do", n, arg)), 1)


def dve_mix(K, dve, s):
    V = mix_views(K)
    dve_norm(K, dve, K.x_res, V["normed"])
    dve.drain().then_inc(K.phase_met, 1)
    dve.wait_ge(K.phase_met, K.phase_end("dve"))
    lb, l0 = V["lb"], K.gains_at["hgrn_lb_logits_2"]
    dve.tensor_tensor(lb[:, 4, :], K.gains[:, l0:l0 + 8], K.gains[:, l0 + 8:l0 + 16], ALU.max).then_inc(K.one_more("dve"), 1)
    dve.wait_ge(K.steps["dve"], K.step_n["dve"])
    dve.tensor_tensor(lb[:, 0, :], K.gains[:, l0:l0 + 8], lb[:, 4, :], ALU.subtract).then_inc(K.one_more("dve"), 1)
    dve.wait_ge(K.steps["dve"], K.step_n["dve"])
    dve.tensor_tensor(lb[:, 1, :], K.gains[:, l0 + 8:l0 + 16], lb[:, 4, :], ALU.subtract).then_inc(K.lb_shifted, 1)
    dve.wait_ge(K.lb_exps, 1)
    dve.tensor_tensor(lb[:, 4, :], lb[:, 2, :], lb[:, 3, :], ALU.add).then_inc(K.one_more("dve"), 1)
    dve.wait_ge(K.steps["dve"], K.step_n["dve"])
    dve.reciprocal(lb[:, 5, :], lb[:, 4, :]).then_inc(K.one_more("dve"), 1)
    dve.wait_ge(K.steps["dve"], K.step_n["dve"])
    for n in range(2):
        dve.tensor_tensor(lb[:, n, :], lb[:, 2 + n, :], lb[:, 5, :], ALU.mult).then_inc(K.one_more("dve"), 1)
        dve.wait_ge(K.steps["dve"], K.step_n["dve"])
    for g in range(2):
        for h in range(4):
            dve.wait_ge(K.free_of(((s, "hf", g), h)), K.turn(((s, "hf", g), h)))
            hh = 4 * g + h
            f = V["w"][:, 0, h * T:(h + 1) * T]
            dve.tensor_scalar(V["k"][:, h, :], V["k"][:, h, :], lb[:, 1, hh:hh + 1], None, ALU.mult).then_inc(K.one_more("dve"), 1)
            ins = dve.tensor_scalar(f, f, lb[:, 1, hh:hh + 1], lb[:, 0, hh:hh + 1], ALU.mult, ALU.add)
            if h < 3:
                ins.then_inc(K.one_more("dve"), 1)
            else:
                ins.then_inc(K.hgrn_f, 1)
        dve.wait_ge(K.hgrn_log_f, g + 1)
        for h in range(4):
            dve.tensor_tensor_scan(V["b"][:, h, :], K.const("scan"), V["w"][:, 0, h * T:(h + 1) * T],
                                                 0.0, ALU.mult, ALU.add).then_inc(K.one_more("dve"), 1)
        dve.wait_ge(K.steps["dve"], K.step_n["dve"])
        b = V["b"].rearrange("p h t -> p (h t)")
        q = V["q"].rearrange("p h t -> p (h t)")
        k = V["k"].rearrange("p h t -> p (h t)")
        for h in range(4):
            dve.wait_ge(K.free_of(((s, "hq", g), h)), K.turn(((s, "hq", g), h)))

        def diffs(lv):
            m = 1 << lv
            bh, wh = halves(b, m), halves(V["w"][:, lv % 2, :], m)
            ref = bh[:, :, 0, m - 1:m].to_broadcast([P, 4 * T // (2 * m), m])
            dve.tensor_tensor(wh[:, :, 1, :], bh[:, :, 1, :], ref, ALU.subtract).then_inc(K.one_more("dve"), 1)
            dve.wait_ge(K.steps["dve"], K.step_n["dve"])
            dve.tensor_tensor(wh[:, :, 0, :], ref, bh[:, :, 0, :], ALU.subtract).then_inc(K.hgrn_diffs, 1)

        def scores(lv):
            for h in range(4):
                key = (s, "hs", g, lv, h)
                dve.wait_ge(K.full_of(key), K.turn(key))
                bank = K.bank(key).rearrange("p (j t) -> p j t", j=NT)
                dst = V["s_t"][:, h * NT:(h + 1) * NT, :]
                mask = K.const("ident" if lv == LEVELS else f"level{lv}")
                if lv == 0:
                    dve.tensor_tensor(dst, bank, over(mask, NT), ALU.mult).then_inc(K.free_of(key), 1)
                else:
                    dve.copy_predicated(dst, over(mask.bitcast(I32), NT), bank).then_inc(K.free_of(key), 1)

        diffs(0)
        diffs(1)
        for lv in range(LEVELS):
            m = 1 << lv
            dve.wait_ge(K.hgrn_decays, g * LEVELS + lv + 1)
            wh = halves(V["w"][:, lv % 2, :], m)
            dve.tensor_tensor(wh[:, :, 1, :], wh[:, :, 1, :], halves(q, m)[:, :, 1, :], ALU.mult).then_inc(K.one_more("dve"), 1)
            dve.wait_ge(K.steps["dve"], K.step_n["dve"])
            dve.tensor_tensor(wh[:, :, 0, :], wh[:, :, 0, :], halves(k, m)[:, :, 0, :], ALU.mult).then_inc(K.hgrn_factors, 1)
            if lv:
                if lv > 1:
                    dve.wait_ge(K.free_of((s, "hs", g, lv - 2, 3)), K.turn((s, "hs", g, lv - 2, 3)))
                scores(lv - 1)
                if lv + 1 < LEVELS:
                    diffs(lv + 1)
        for lv in (LEVELS - 1, LEVELS):
            dve.wait_ge(K.free_of((s, "hs", g, lv - 1, 3)), K.turn((s, "hs", g, lv - 1, 3)))
            scores(lv)
        dve.drain().then_inc(K.phase_met, 1)
        dve.wait_ge(K.phase_met, K.phase_end("dve"))
        ends = V["b"].rearrange("p h (c i) -> p (h c) i", i=CH)
        dve.tensor_tensor(V["w"][:, 1, :].rearrange("p (c i) -> p c i", i=CH),
                                 ends[:, :, CH - 1:CH].to_broadcast([P, 4 * NC, CH]), ends, ALU.subtract).then_inc(K.hgrn_to_end, 1)
        dve.wait_ge(K.hgrn_end_decays, g + 1)
        dve.tensor_tensor(V["w"][:, 1, :], V["w"][:, 1, :], k, ALU.mult).then_inc(K.hgrn_k_to_end, 1)
        dve.tensor_tensor(V["w"][:, 0, :], V["w"][:, 0, :], q, ALU.mult).then_inc(K.one_more("dve"), 1)
        dve.memset(V["state"].rearrange("p (h c) e -> p h c e", h=4)[:, :, 0, :], 0.0).then_inc(K.one_more("dve"), 1)
        for c in range(NC - 1):
            for h in range(4):
                dve.wait_ge(K.full_of((s, "hu", g, h, c % 2)), K.turn((s, "hu", g, h, c % 2)))
                bank = K.bank((s, "hu", g, h, c % 2))
                u = bank[:, (c // 2) * P:(c // 2 + 1) * P]
                nxt = V["state"][:, h * NC + c + 1, :]
                if c == 0:
                    ins = dve.tensor_copy(nxt, u)
                else:
                    ins = dve.scalar_tensor_tensor(nxt, V["state"][:, h * NC + c, :],
                                                   V["b_end"][:, 0, h * NC + c:h * NC + c + 1], u, ALU.mult, ALU.add)
                ins.then_inc(K.one_more("dve"), 1)
            dve.wait_ge(K.steps["dve"], K.step_n["dve"])
        for h in range(4):
            for par in range(2):
                ins = dve.tensor_copy(K.stat[:, 76:77], K.stat[:, 77:78])
                ins.then_inc(K.free_of((s, "hu", g, h, par)), 1)
                dve.wait_ge(K.free_of((s, "hu", g, h, par)), K.turn((s, "hu", g, h, par)))
        dve.tensor_copy(K.stat[:, 76:77], K.stat[:, 77:78]).then_inc(K.hgrn_states, 1)
        dve_head_norm(K, dve, V["o"], g * 512, 128, V["gate"], K.hgrn_squares, g + 1,
                      K.hgrn_gated)
        dve.drain().then_inc(K.phase_met, 1)
        dve.wait_ge(K.phase_met, K.phase_end("dve"))
    for half in range(2):
        for t in range(NT):
            dve.wait_ge(K.free_of(((s, "gate_h", half), t)), K.turn(((s, "gate_h", half), t)))
            key = ((s, "y_h"), half, t)
            c = slice(half * 512, (half + 1) * 512)
            dve.wait_ge(K.full_of(key), K.turn(key))
            dve.tensor_tensor(V["y"][:, t, c], V["gate_y"][:, t, c], K.bank(key), ALU.mult).then_inc(K.free_of(key), 1)
    dve.wait_ge(K.free_of(((s, "y_h"), 1, NT - 1)), K.turn(((s, "y_h"), 1, NT - 1)))
    for t in range(NT - 1):
        dve.wait_ge(K.free_of(((s, "y_h"), 1, t)), K.turn(((s, "y_h"), 1, t)))
    dve.tensor_copy(K.stat[:, 76:77], K.stat[:, 77:78]).then_inc(K.y_h_ready, 1)
    dve.wait_ge(K.y_spilled, 16)
    dve.drain().then_inc(K.phase_met, 1)
    dve.wait_ge(K.phase_met, K.phase_end("dve"))
    raw, gd = V["gd_raw"], V["gd"]
    g4 = lambda i: gd[:, i, :].rearrange("p (t v) -> p t v", t=NT)
    dve.tensor_tensor(g4(1), raw[:, :, 0:16], over(K.small_rows[:, 400:416], NT), ALU.add).then_inc(K.softplus_in, 1)
    dve.wait_ge(K.softplus_exp, 1)
    dve.tensor_scalar(gd[:, 3, :], gd[:, 3, :], 1.0, None, ALU.add).then_inc(K.softplus_one, 1)
    dve.wait_ge(K.softplus_ln, 1)
    dve.scalar_tensor_tensor(gd[:, 3, :], gd[:, 1, :], 0.0, gd[:, 3, :], ALU.max, ALU.add).then_inc(K.one_more("dve"), 1)
    dve.wait_ge(K.steps["dve"], K.step_n["dve"])
    dve.tensor_tensor(g4(3), g4(3), over(V["sc16"], NT), ALU.mult).then_inc(K.one_more("dve"), 1)
    dve.wait_ge(K.steps["dve"], K.step_n["dve"])
    dve.tensor_scalar(gd[:, 0, :], gd[:, 3, :], -1.0, None, ALU.mult).then_inc(K.gdn_decays, 1)
    dve.wait_ge(K.free_of((s, "gam")), K.turn((s, "gam")))
    dve.tensor_scalar(gd[:, 5, :], gd[:, 5, :], -1.0, None, ALU.mult).then_inc(K.one_more("dve"), 1)
    dve.wait_ge(K.steps["dve"], K.step_n["dve"])
    for g in range(4):
        dve.memset(V["pad"][:, :, 0:3], 0.0).then_inc(K.one_more("dve"), 1)
        dve.wait_ge(K.steps["dve"], K.step_n["dve"])
        for n in range(8):
            dve.wait_ge(K.free_of(((s, "gqk", g), n) if n < 4 else ((s, "gv", g), n - 4)), K.turn(((s, "gqk", g), n) if n < 4 else ((s, "gv", g), n - 4)))
            if n >= 4:
                dve.wait_ge(K.conv_silu, 8 * g + n - 3)
            tile = (2 * g + n, 8 + 2 * g + n - 2)[n >= 2] if n < 4 else 16 + 4 * g + n - 4
            acc, x = V["acc"][:, n % 4, :], V["pad"][:, n % 4, :]
            w = lambda i: K.conv_w[:, 32 * i + tile:32 * i + tile + 1]
            dve.tensor_scalar(acc, x[:, 0:T], w(0), None, ALU.mult).then_inc(K.one_more("dve"), 1)
            dve.wait_ge(K.steps["dve"], K.step_n["dve"])
            for i in range(1, 3):
                dve.scalar_tensor_tensor(acc, x[:, i:T + i], w(i), acc, ALU.mult, ALU.add).then_inc(K.one_more("dve"), 1)
                dve.wait_ge(K.steps["dve"], K.step_n["dve"])
            dve.scalar_tensor_tensor(acc, x[:, 3:T + 3], w(3), acc, ALU.mult, ALU.add).then_inc(K.conv_done, 1)
        dve.drain().then_inc(K.phase_met, 1)
        dve.wait_ge(K.phase_met, K.phase_end("dve"))
        for m in range(2):
            dve.wait_ge(K.free_of((s, "qk_sum", g, m)), K.turn((s, "qk_sum", g, m)))
            dve.reciprocal(V["pad"][:, m, 0:T], V["pad"][:, m, 0:T]).then_inc(K.qk_inverted, 1)
        for n in range(4):
            dve.wait_ge(K.full_of((s, "qk_scale", g, n)), K.turn((s, "qk_scale", g, n)))
            dve.scalar_tensor_tensor(V["c_qk"][:, n, :], V["c_qk"][:, n, :], DK ** -0.5 if n < 2 else 1.0,
                                     K.bank((s, "qk_scale", g, n)), ALU.mult,
                                     ALU.mult).then_inc(K.free_of((s, "qk_scale", g, n)), 1)
        dve.drain().then_inc(K.phase_met, 1)
        dve.wait_ge(K.phase_met, K.phase_end("dve"))
        dve.memset(V["m_s"], 0.0).then_inc(K.one_more("dve"), 1)
        dve.wait_ge(K.steps["dve"], K.step_n["dve"])
        for j, piece, arg in delta_order():
            dve_delta_piece(K, dve, s, V, g, j, piece, arg)
        dve.drain().then_inc(K.phase_met, 1)
        dve.wait_ge(K.phase_met, K.phase_end("dve"))
        dve_head_norm(K, dve, V["o_tok"], 0, 256, V["z"], K.gdn_squares, g + 1, K.gdn_gated)
        dve.wait_ge(K.free_of((s, "og_t", g, 3)), K.turn((s, "og_t", g, 3)))
    dve.tensor_copy(K.stat[:, 76:77], K.stat[:, 77:78]).then_inc(K.y_h_wanted, 1)
    dve.drain().then_inc(K.phase_met, 1)
    dve.wait_ge(K.phase_met, K.phase_end("dve"))
    dve.wait_ge(K.y_reloaded, 16)
    for half in range(2):
        for t in range(NT):
            dve.wait_ge(K.free_of(((s, "gate_g", half), t)), K.turn(((s, "gate_g", half), t)))
            key = ((s, "y_g"), half, t)
            c = slice(half * 512, (half + 1) * 512)
            y = V["y2"][:, t, c]
            dve.wait_ge(K.full_of(key), K.turn(key))
            dve.tensor_tensor(y, V["gate_g"][:, t, c], K.bank(key), ALU.mult).then_inc(K.free_of(key), 1)
            dve.wait_ge(K.free_of(key), K.turn(key))
            ins = dve.tensor_tensor(y, y, V["y_h"][:, t, c], ALU.add)
            if (half, t) != (1, NT - 1):
                ins.then_inc(K.one_more("dve"), 1)
                dve.wait_ge(K.steps["dve"], K.step_n["dve"])
            else:
                ins.then_inc(K.branches_added, 1)
    for half in range(2):
        for t in range(NT):
            key = ((s, "out"), half, t)
            x = K.x_res[:, t, half * BANK:(half + 1) * BANK]
            dve.wait_ge(K.full_of(key), K.turn(key))
            dve.tensor_tensor(x, x, K.bank(key), ALU.add).then_inc(K.free_of(key), 1)
    dve.drain().then_inc(K.phase_met, 1)
    dve.wait_ge(K.phase_met, K.phase_end("dve"))


def dve_head_norm(K, dve, o, col, gain, gate, squares, n_squares, done):
    dve.wait_ge(squares, n_squares)
    dve.reciprocal(K.stat[:, 112:128], K.stat[:, 96:112]).then_inc(K.one_more("dve"), 1)
    dve.wait_ge(K.steps["dve"], K.step_n["dve"])
    for t in range(NT):
        for h in range(4):
            n = t * 4 + h
            x = o[:, t, col + h * P:col + (h + 1) * P]
            dve.scalar_tensor_tensor(x, x, K.stat[:, 112 + n:113 + n], K.small_rows[:, gain:gain + P],
                                                   ALU.mult, ALU.mult).then_inc(K.one_more("dve"), 1)
    dve.wait_ge(K.steps["dve"], K.step_n["dve"])
    for t in range(NT):
        x = o[:, t, col:col + 512]
        ins = dve.tensor_tensor(x, x, gate[:, t, :], ALU.mult)
        if t == NT - 1 and done:
            ins.then_inc(done, 1)
        else:
            ins.then_inc(K.one_more("dve"), 1)
            dve.wait_ge(K.steps["dve"], K.step_n["dve"])


def dve_delta_piece(K, dve, s, V, g, j, piece, arg):
    n = g * NT + j
    ts = slice(j * P, (j + 1) * P)
    gd = V["gd"]
    col = lambda i, v: gd[:, i, j * 16 + 4 * g + v:j * 16 + 4 * g + v + 1]
    lt = V["m_lt"]
    if piece == "decays":
        dve.wait_ge(K.free_of((s, "gb", n)), K.turn((s, "gb", n)))
        for v in range(4):
            ins = dve.tensor_scalar(lt[:, v, :], V["m_gb"][:, v, :], col(4, v), 0.0, ALU.subtract, ALU.min)
            if v < 3:
                ins.then_inc(K.one_more("dve"), 1)
            else:
                ins.then_inc(K.gdn_diff, 1)
    if piece == "prepare":
        dve.wait_ge(K.gdn_decay, n + 1)
        dve.tensor_copy(V["sc"][0:CH, 0, 0:4], lt[0:CH, :, CH - 1]).then_inc(K.one_more("dve"), 1)
        dve.wait_ge(K.steps["dve"], K.step_n["dve"])
        dve.tensor_copy(V["sc"][CH:P, 0, 0:4], lt[CH:P, :, P - 1]).then_inc(K.end_scales, 1)
        dve.wait_ge(K.end_scales, n + 1)
        dve.tensor_tensor(lt, lt, over(K.const("cum"), 4), ALU.mult).then_inc(K.one_more("dve"), 1)
        dve.wait_ge(K.steps["dve"], K.step_n["dve"])
        dve.wait_ge(K.full_of((s, "kq", n)), K.turn((s, "kq", n)))
        bank = K.bank((s, "kq", n)).rearrange("p (m t) -> p m t", m=4)
        lt2 = lt.rearrange("p (m r) t -> p m r t", r=2)
        two = lambda ap: ap.unsqueeze(2).to_broadcast([P, 2, 2, P])
        dve.tensor_tensor(V[f"m_qk{n % 2}"].rearrange("p (m r) t -> p m r t", r=2), two(bank[:, 2:4, :]), lt2,
                                        ALU.mult).then_inc(K.one_more("dve"), 1)
        dve.wait_ge(K.steps["dve"], K.step_n["dve"])
        dve.tensor_tensor(V["m_at"].rearrange("p (m r) t -> p m r t", r=2), two(bank[:, 0:2, :]), lt2, ALU.mult).then_inc(K.free_of((s, "kq", n)), 1)
        dve.wait_ge(K.free_of((s, "kq", n)), K.turn((s, "kq", n)))
        for v in range(4):
            dve.tensor_scalar(V["m_at"][:, v, :], V["m_at"][:, v, :], col(2, v), None, ALU.mult).then_inc(K.one_more("dve"), 1)
        dve.wait_ge(K.steps["dve"], K.step_n["dve"])
        dve.tensor_tensor(V["m_al0"], V["m_at"], over(K.const("level0"), 4), ALU.mult).then_inc(K.one_more("dve"), 1)
        dve.wait_ge(K.steps["dve"], K.step_n["dve"])
        dve.tensor_tensor(V[f"m_rr{n % 2}"], over(K.const("ident"), 4), V["m_al0"], ALU.subtract).then_inc(K.rr_ready, 1)
        dve.wait_ge(K.rr_ready, n + 1)
        dve.tensor_tensor(V["m_al1"], V["m_at"], over(K.const("level1"), 4), ALU.mult).then_inc(K.level_ready, 1)
        dve.tensor_tensor(V[f"m_qe{n % 2}"].rearrange("p (m r) t -> p m r t", r=2), two(V["c_qk"][:, 0:2, ts]),
                                        V[f"m_eg{n % 2}"].rearrange("p (m r) t -> p m r t", r=2), ALU.mult).then_inc(K.one_more("dve"), 1)
        dve.wait_ge(K.steps["dve"], K.step_n["dve"])
        dve.tensor_copy(K.stat[:, 76:77], K.stat[:, 77:78]).then_inc(K.qe_ready, 1)
    if piece == "level":
        lv = arg
        if lv + 1 < LEVELS:
            if lv > 1:
                dve.wait_ge(K.full_of((s, "tx", n, lv - 1)), K.turn((s, "tx", n, lv - 1)))
            dve.tensor_tensor(V[f"m_al{(lv + 1) % 2}"], V["m_at"], over(K.const(f"level{lv + 1}"), 4),
                                     ALU.mult).then_inc(K.level_ready, 1)
    if piece == "doubled":
        lv = arg
        if lv == 1:
            dve.wait_ge(K.free_of((s, "t0", n)), K.turn((s, "t0", n)))
        if lv + 1 < LEVELS:
            key = (s, "ty", n, lv)
            dve.wait_ge(K.full_of(key), K.turn(key))
            bank = K.bank(key).rearrange("p (v t) -> p v t", v=4)
            dve.tensor_tensor(V["m_tt"], V["m_tt"], bank, ALU.subtract).then_inc(K.free_of(key), 1)
            dve.wait_ge(K.free_of(key), K.turn(key))
        key = (s, "ry", n, lv)
        dve.wait_ge(K.full_of(key), K.turn(key))
        bank = K.bank(key).rearrange("p (v t) -> p v t", v=4)
        dve.tensor_tensor(V[f"m_rr{n % 2}"], V[f"m_rr{n % 2}"], bank, ALU.subtract).then_inc(K.free_of(key), 1)
        dve.wait_ge(K.free_of(key), K.turn(key))
    if piece == "keys":
        for v in range(4):
            ins = dve.tensor_scalar(V["m_rn"][:, v, :], V[f"m_rr{n % 2}"][:, v, :], col(5, v), None, ALU.mult)
            if v < 3:
                ins.then_inc(K.one_more("dve"), 1)
            else:
                ins.then_inc(K.rn_ready, 1)
    if piece == "values":
        c = arg
        ps = slice(CH * c, CH * (c + 1))
        key = (s, "vn", n, c)
        dve.wait_ge(K.full_of(key), K.turn(key))
        bank = K.bank(key).rearrange("p (v t) -> p v t", v=4)
        c0 = j * 16 + 4 * g
        beta = gd[ps, 2, c0:c0 + 4].unsqueeze(2).to_broadcast([CH, 4, P])
        dve.tensor_tensor(V["m_vn"][ps, :, :], bank[ps, :, :], beta, ALU.mult).then_inc(K.free_of(key), 1)
    if piece == "state":
        c = arg
        dve.wait_ge(K.full_of((s, "do", n, c)), K.turn((s, "do", n, c)))
        key = (s, "su", n, c)
        dve.wait_ge(K.full_of(key), K.turn(key))
        bank = K.bank(key)
        end = CH * (c + 1) - 1
        for v in range(4):
            ins = dve.scalar_tensor_tensor(V["m_s"][:, v, :], V["m_s"][:, v, :], V[f"m_eg{n % 2}"][:, v, end:end + 1],
                                           bank[:, v * P:(v + 1) * P], ALU.mult, ALU.add)
            if v < 3:
                ins.then_inc(K.one_more("dve"), 1)
                dve.wait_ge(K.steps["dve"], K.step_n["dve"])
            else:
                ins.then_inc(K.free_of(key), 1)
                dve.wait_ge(K.free_of(key), K.turn(key))

def act_final(K, act):
    _, _, _, junk = ffn_views(K)
    act_norm(K, act, K.x_res, junk)


def dve_final(K, dve):
    n = K.norm_n["dve"]
    dve.wait_ge(K.squares_summed, n + 1)
    dve.reciprocal(K.stat[:, 4:4 + NT], K.stat[:, 0:NT]).then_inc(K.one_more("dve"), 1)
    dve.wait_ge(K.steps["dve"], K.step_n["dve"])
    K.rows_landed += 16
    dve.wait_ge(K.row_landed, K.rows_landed)
    final, _ = K.carve(0, NT, D)
    for t in range(NT):
        dve.scalar_tensor_tensor(final[:, t, :], K.x_res[:, t, :], K.stat[:, 4 + t:5 + t], K.row[:],
                                        ALU.mult, ALU.mult).then_inc(K.final_rows, 1)


def sp_final(K, sp):
    final, _ = K.carve(0, NT, D)
    for t in range(NT):
        sp.wait_ge(K.final_rows, t + 1)
        sp.dma_start(K.out[0, t * P:(t + 1) * P, :], final[:, t, :]).then_inc(K.output_stored, 16)
    sp.wait_ge(K.output_stored, 16 * NT)


PE_STAGES = {"even": pe_even, "odd": pe_odd, "ffn1": pe_ffn, "mix": pe_mix, "ffn2": pe_ffn}
ACT_STAGES = {"even": act_even, "odd": act_odd, "ffn1": act_ffn, "mix": act_mix, "ffn2": act_ffn}
DVE_STAGES = {"even": dve_even, "odd": dve_odd, "ffn1": dve_ffn, "mix": dve_mix, "ffn2": dve_ffn}
STAGES = ("even", "odd", "ffn1", "mix", "ffn2")
ROW_OF = {"even": ("post_norm", 0), "odd": ("post_norm", 1)}


def build(nc, A, out, stages=STAGES):
    with ExitStack() as ctx:
        K = Program(nc, ctx, A, out, stages)
        K.eps = ctx.enter_context(nc.sbuf_tensor("eps", [P, 1], F32))
        K.trig = ctx.enter_context(nc.sbuf_tensor("trig", [P, 2, NT * 48], F32))
        K.gd_raw = ctx.enter_context(nc.sbuf_tensor("delta_raw", [P, NT, 32], F32))
        K.sc16 = ctx.enter_context(nc.sbuf_tensor("delta_rates", [P, 16], F32))
        K.y_dram = nc.dram_tensor("y_spill", [P, NT, D], F32).ap() if "mix" in stages else None
        K.y_spilled, K.y_reloaded = K.sem("y_spilled"), K.sem("y_reloaded")
        K.lam = ctx.enter_context(nc.sbuf_tensor("lam", [P, 8], F32))
        K.norm_n = {"pe": 0, "dve": 0}
        K.rows_landed = 0
        K.rows_used = 0
        K.att_base, base = {}, 0
        for s, tags in (("even", "a"), ("odd", "cm")):
            for tag in tags if s in stages else "":
                K.att_base[tag] = base
                base += 8 * NT
        block = ctx.enter_context(nc.Block())

        @block.tensor
        def _(pe):
            pe_setup(K, pe)
            for s in stages:
                PE_STAGES[s](K, pe, s)

        @block.scalar
        def _(act):
            act_setup(K, act)
            for s in stages:
                ACT_STAGES[s](K, act, s)
            act_final(K, act)

        @block.vector
        def _(dve):
            dve_setup(K, dve)
            for s in stages:
                DVE_STAGES[s](K, dve, s)
            dve_final(K, dve)

        @block.sync
        def _(sp):
            sp_setup(K, sp)
            for i, blk in enumerate(K.blocks):
                if i >= SLOTS:
                    sp.wait_ge(K.weights_used, i - SLOTS + 2)
                slot = K.ring[:, i % SLOTS]
                for at, src in blk:
                    if at == "uq":
                        dst = slot[:, 0:3, :].rearrange("p a b -> p (a b)").rearrange("p (k c) -> p k c", k=2)
                    elif at == "ukv":
                        dst = slot[:, 3:5, :].rearrange("p a b -> p (a b)")
                    else:
                        dst = slot[:, 0:src.shape[1], at:at + src.shape[2]]
                    sp.dma_start(dst, src).then_inc(K.weight_landed[i % SLOTS], 16)
            sp_final(K, sp)

        @block.gpsimd
        def _(pool):
            rows = [ROW_OF[s] for s in stages if s in ROW_OF] + [("final_norm_2", None)]
            for n, (name, i) in enumerate(rows):
                if n == len(rows) - 1 and "mix" in stages:
                    V = mix_views(K)
                    pool.wait_ge(K.y_h_ready, 1)
                    pool.dma_start(K.y_dram, V["y"]).then_inc(K.y_spilled, 16)
                    pool.wait_ge(K.y_h_wanted, 1)
                    pool.wait_ge(K.y_spilled, 16)
                    pool.dma_start(V["y_h"], K.y_dram).then_inc(K.y_reloaded, 16)
                if n:
                    pool.wait_ge(K.row_used, n)
                src = K.A[name][i:i + 1, :] if i is not None else K.A[name].rearrange("(a d) -> a d", a=1)
                pool.dma_start(K.row[:], src.to_broadcast([P, D])).then_inc(K.row_landed, 16)


_INS = ["x", "positions", "pre_norm", "post_norm", "w_in_even", "w_out_even", "w_in_odd", "diff_lambda",
        "diff_subln", "mla_q_norm", "mla_kv_norm", "mla_w_uq", "mla_w_ukv", "w_out_odd", "ffn1_norm_2",
        "ffn1_w_in_2", "ffn1_w_out_2", "mix_norm_2", "w_in_2", "hgrn_lb_logits_2", "hgrn_out_norm_2",
        "gdn_conv_w_2", "gdn_a_log_2", "gdn_dt_bias_2", "gdn_out_norm_2", "w_branch_hgrn_2", "w_branch_gdn_2",
        "w_out_2", "ffn2_norm_2", "ffn2_w_in_2", "ffn2_w_out_2", "final_norm_2"]


def kernel(**inputs):
    import concourse.bacc as _bacc
    from concourse.bass_utils import run_bass_kernel_spmd as _run

    nc = _bacc.Bacc("TRN2", target_bir_lowering=False, num_devices=1)
    arrays, aps = {}, {}
    for name in _INS + ["consts"]:
        a = constants()[0] if name == "consts" else np.ascontiguousarray(inputs[name])
        arrays[f"in_{name}_dram"] = a
        aps[name] = nc.dram_tensor(f"in_{name}_dram", a.shape, mybir.dt.from_np(a.dtype), kind="ExternalInput").ap()
    out = nc.dram_tensor("out_0_dram", (1, T, D), F32, kind="ExternalOutput").ap()
    build(nc, aps, out)
    r = _run(nc, [arrays], core_ids=[0])
    return r.results[0]["out_0_dram"]
```
